# Optimizing a Trainium2 kernel written in Bass

```python
import jax, jax.numpy as jnp
from jax import lax
import numpy as np

D_MODEL = 2048
BATCH = 1
SEQ = 256
DEPTH = 1

SG_GROUPS = 8
SG_GROUP_DIM = 128
SG_WIDTH = SG_GROUPS * SG_GROUP_DIM
SG_CHUNK = 128
N_HEADS = 8
N_KV_HEADS = 2
HEAD_DIM = 128
Q_PER_KV = N_HEADS // N_KV_HEADS
Q_WIDTH = N_HEADS * HEAD_DIM
KV_WIDTH = N_KV_HEADS * HEAD_DIM
WINDOW = 128
BLOCK = 128
ROPE_THETA = 500000.0
ROT_DIM = HEAD_DIM // 4
N_BRANCHES = 2
D_FF = 5632
CONV_WIDTH = 3
EPS = 1e-6
MASK_VALUE = -1e30

IN_WIDTH = 2 * SG_WIDTH + Q_WIDTH + 2 * KV_WIDTH + N_BRANCHES * D_MODEL

kernel_name = "hybrid_sgmlp_swa_sink_convffn_block"

def rms_norm(x, g):
    xf = x.astype(jnp.float32)
    y = xf * lax.rsqrt(jnp.mean(xf * xf, axis=-1, keepdims=True) + EPS)
    return (y * g.astype(jnp.float32)).astype(x.dtype)

def layer_norm(x, g, b):
    xf = x.astype(jnp.float32)
    mu = jnp.mean(xf, axis=-1, keepdims=True)
    xc = xf - mu
    y = xc * lax.rsqrt(jnp.mean(xc * xc, axis=-1, keepdims=True) + EPS)
    return (y * g.astype(jnp.float32) + b.astype(jnp.float32)).astype(x.dtype)

def partial_rope(x):
    s = x.shape[1]
    pos = jnp.arange(s, dtype=jnp.float32)
    inv_freq = ROPE_THETA ** (-jnp.arange(0, ROT_DIM, 2, dtype=jnp.float32) / ROT_DIM)
    ang = pos[:, None] * inv_freq[None, :]
    cos = jnp.cos(ang)[None, :, None, :]
    sin = jnp.sin(ang)[None, :, None, :]
    xf = x.astype(jnp.float32)
    x1 = xf[..., : ROT_DIM // 2]
    x2 = xf[..., ROT_DIM // 2: ROT_DIM]
    rot = jnp.concatenate([x1 * cos - x2 * sin, x2 * cos + x1 * sin, xf[..., ROT_DIM:]], axis=-1)
    return rot.astype(x.dtype)

def spatial_gating(u, v, ln_g, ln_b, w_s, b_s):
    b, s, _ = v.shape
    nc = s // SG_CHUNK
    vn = layer_norm(v, ln_g, ln_b).reshape(b, nc, SG_CHUNK, SG_GROUPS, SG_GROUP_DIM)
    vz = jnp.einsum('gts,bcsgd->bctgd', w_s, vn) + b_s.T[None, None, :, :, None]
    return u * vz.reshape(b, s, SG_WIDTH)

def banded_blocks(t):
    b, s, kvh, d = t.shape
    nb = s // BLOCK
    tp = jnp.pad(t, ((0, 0), (BLOCK, BLOCK), (0, 0), (0, 0))).reshape(b, nb + 2, BLOCK, kvh, d)
    return jnp.concatenate([tp[:, :-2], tp[:, 1:-1], tp[:, 2:]], axis=2)

def windowed_gqa_sink(q, k, v, sink):
    b, s, _, _ = q.shape
    nb = s // BLOCK
    qb = q.reshape(b, nb, BLOCK, N_KV_HEADS, Q_PER_KV, HEAD_DIM)
    kb = banded_blocks(k)
    vb = banded_blocks(v)
    scores = jnp.einsum('bnqkgd,bnskd->bkgnqs', qb, kb).astype(jnp.float32) * (HEAD_DIM ** -0.5)
    blk = jnp.arange(nb)[:, None, None]
    q_pos = blk * BLOCK + jnp.arange(BLOCK)[None, :, None]
    k_pos = blk * BLOCK - BLOCK + jnp.arange(3 * BLOCK)[None, None, :]
    valid = (jnp.abs(k_pos - q_pos) <= WINDOW) & (k_pos >= 0) & (k_pos < s)
    scores = jnp.where(valid, scores, MASK_VALUE)
    sink_l = jnp.broadcast_to(
        sink.astype(jnp.float32).reshape(N_KV_HEADS, Q_PER_KV)[None, :, :, None, None, None],
        scores.shape[:-1] + (1,))
    probs = jax.nn.softmax(jnp.concatenate([scores, sink_l], axis=-1), axis=-1)[..., :-1]
    out = jnp.einsum('bkgnqs,bnskd->bnqkgd', probs.astype(v.dtype), vb)
    return out.reshape(b, s, Q_WIDTH)

def conv_glu_ffn(h, w_up, conv_w, conv_b, w_down):
    s = h.shape[1]
    up = h @ w_up
    pad = CONV_WIDTH // 2
    up_p = jnp.pad(up, ((0, 0), (pad, pad), (0, 0)))
    conv = conv_b + sum(conv_w[j] * up_p[:, j:j + s] for j in range(CONV_WIDTH))
    gate, val = jnp.split(conv, 2, axis=-1)
    return (jax.nn.gelu(gate, approximate=True) * val) @ w_down

def setup_inputs(seed: int = 0) -> dict:
    key = jax.random.key(seed)
    ks = jax.random.split(key, 20)
    f32 = jnp.float32

    def nrm(k, shape, scale):
        return jax.random.normal(k, shape, f32) * scale

    def gain(k, n):
        return 1.0 + 0.05 * jax.random.normal(k, (DEPTH, n), f32)

    return {
        "x": nrm(ks[0], (BATCH, SEQ, D_MODEL), 1.0),
        "norm_mix_pre": gain(ks[1], D_MODEL),
        "w_in": nrm(ks[2], (DEPTH, D_MODEL, IN_WIDTH), D_MODEL ** -0.5),
        "sg_ln_g": gain(ks[3], SG_WIDTH),
        "sg_ln_b": nrm(ks[4], (DEPTH, SG_WIDTH), 0.02),
        "sg_w": nrm(ks[5], (DEPTH, SG_GROUPS, SG_CHUNK, SG_CHUNK), SG_CHUNK ** -0.5),
        "sg_b": 1.0 + nrm(ks[6], (DEPTH, SG_GROUPS, SG_CHUNK), 0.05),
        "attn_sink": nrm(ks[7], (DEPTH, N_HEADS), 1.0),
        "w_branch_a": nrm(ks[8], (DEPTH, SG_WIDTH, D_MODEL), SG_WIDTH ** -0.5),
        "w_branch_b": nrm(ks[9], (DEPTH, Q_WIDTH, D_MODEL), Q_WIDTH ** -0.5),
        "w_out": nrm(ks[10], (DEPTH, D_MODEL, D_MODEL), D_MODEL ** -0.5),
        "norm_mix_post": gain(ks[11], D_MODEL),
        "norm_ffn_pre": gain(ks[12], D_MODEL),
        "w_up": nrm(ks[13], (DEPTH, D_MODEL, 2 * D_FF), D_MODEL ** -0.5),
        "conv_w": nrm(ks[14], (DEPTH, CONV_WIDTH, 2 * D_FF), CONV_WIDTH ** -0.5),
        "conv_b": nrm(ks[15], (DEPTH, 2 * D_FF), 0.01),
        "w_down": nrm(ks[16], (DEPTH, D_FF, D_MODEL), D_FF ** -0.5),
        "norm_ffn_post": gain(ks[17], D_MODEL),
    }

def reference(x, norm_mix_pre, w_in, sg_ln_g, sg_ln_b, sg_w, sg_b, attn_sink,
              w_branch_a, w_branch_b, w_out, norm_mix_post, norm_ffn_pre,
              w_up, conv_w, conv_b, w_down, norm_ffn_post):
    b, s, _ = x.shape
    split_at = np.cumsum([SG_WIDTH, SG_WIDTH, Q_WIDTH, KV_WIDTH, KV_WIDTH]).tolist()
    for l in range(DEPTH):
        h = rms_norm(x, norm_mix_pre[l])
        z = h @ w_in[l]
        u, v, q, k, vv, g = jnp.split(z, split_at, axis=-1)
        a_out = spatial_gating(jax.nn.gelu(u, approximate=True), jax.nn.gelu(v, approximate=True),
                               sg_ln_g[l], sg_ln_b[l], sg_w[l], sg_b[l])
        q = partial_rope(q.reshape(b, s, N_HEADS, HEAD_DIM))
        k = partial_rope(k.reshape(b, s, N_KV_HEADS, HEAD_DIM))
        vv = vv.reshape(b, s, N_KV_HEADS, HEAD_DIM)
        b_out = windowed_gqa_sink(q, k, vv, attn_sink[l])
        gates = jax.nn.sigmoid(g.reshape(b, s, N_BRANCHES, D_MODEL))
        merged = gates[:, :, 0] * (a_out @ w_branch_a[l]) + gates[:, :, 1] * (b_out @ w_branch_b[l])
        x = x + rms_norm(merged @ w_out[l], norm_mix_post[l])
        hf = rms_norm(x, norm_ffn_pre[l])
        f = conv_glu_ffn(hf, w_up[l], conv_w[l], conv_b[l], w_down[l])
        x = x + rms_norm(f, norm_ffn_post[l])
    return x


_drawn_inputs = setup_inputs


def setup_inputs(seed=0):
    import zlib

    import numpy as np

    out = dict(_drawn_inputs(seed))
    spreads = {}
    factors = {'sg_ln_b': 5.192, 'attn_sink': 42.656, 'conv_b': 6.996}
    for name, (base, spread) in spreads.items():
        noise = np.random.default_rng([zlib.crc32(name.encode()), seed]).standard_normal(out[name].shape)
        drawn = base * np.exp(spread * noise) if base else spread * noise
        out[name] = __import__('jax').numpy.asarray(drawn.astype(out[name].dtype))
    for name, factor in factors.items():
        out[name] = (out[name] * factor).astype(out[name].dtype)
    return out
```

```python
import concourse.bass as bass
from concourse import mybir

P = 128
D = 2048
SEQ = 256
NT = SEQ // P
KD = D // P
SGW = 1024
NG = SGW // P
NH = 8
NKV = 2
QPK = NH // NKV
DFF = 5632
KF = DFF // P
HALF = KF // 2
ROT = 32
ROPE_THETA = 500000.0
EPS = 1e-6
MASK_VALUE = -1e30
SCALE = float(P) ** -0.5
UNIT = 2048
RING = 4
BLK = 512
NB = D // BLK

T_V, T_KV, T_QU, T_MG, T_OUT, T_FFN = 0, 2, 3, 7, 19, 23
UP_TURNS = KF * 2 // 2 // RING
DOWN_UNITS = HALF // 2
DOWN_TURNS = -(-DOWN_UNITS // RING)
HALF_TURNS = UP_TURNS + 2 * DOWN_TURNS
T_END = T_FFN + 2 * HALF_TURNS
N_UNITS = 224
DOWN_STARTS = [T_FFN + UP_TURNS + h * HALF_TURNS + n * DOWN_TURNS for h in range(2) for n in range(2)]
SHORT_TURNS = [t + DOWN_TURNS - 1 for t in DOWN_STARTS]


def skipped(turn):
    return sum(t < turn for t in SHORT_TURNS)


def exists(turn, slot):
    return turn < T_END and not (slot == RING - 1 and turn in SHORT_TURNS)


def counts_for(turn, slot):
    return 1 if exists(turn, slot + 1) or slot == RING - 1 else 2


def build(nc, x, weights, gains, sg_gb, sg_wT, sg_b, sink, conv, ident_in, mask_in, rope_in, out):
    F32, F32R = mybir.dt.float32, mybir.dt.float32r
    ALU, ACT, AX = mybir.AluOpType, mybir.ActivationFunctionType, mybir.AxisListType

    KB = 1024
    base = 1152
    at = {}

    def region(name, size):
        at[name] = region.top
        region.top += size
    region.top = base
    region("w_hi", RING * 8 * KB)
    region("w_lo", RING * 8 * KB)
    region("raw", RING * 8 * KB)
    region("hT", 32 * KB)
    region("A", 32 * KB)
    region("B", 44 * KB)
    region("gain", 8 * KB)
    region("tmp", 8 * KB)
    region("misc", 2 * KB + 256)

    def sb(name, where, off, shape, dt=F32):
        return nc.alloc_sbuf_tensor_at(name, shape, dt, offset=at[where] + off)

    w_hi = [sb(f"w_hi{s}", "w_hi", s * 8 * KB, [P, UNIT], F32R) for s in range(RING)]
    w_lo = [sb(f"w_lo{s}", "w_lo", s * 8 * KB, [P, UNIT], F32R) for s in range(RING)]
    raw = [sb(f"raw{s}", "raw", s * 8 * KB, [P, UNIT]) for s in range(RING)]
    hT_hi = sb("hT_hi", "hT", 0, [P, KD, SEQ], F32R)
    hT_lo = sb("hT_lo", "hT", 16 * KB, [P, KD, SEQ], F32R)
    xn = sb("xn", "A", 0, [P, NT, D])
    x_tok = sb("x_tok", "A", 16 * KB, [P, NT, D])
    aT_hi = sb("aT_hi", "A", 0, [P, NG, SEQ], F32R)
    aT_lo = sb("aT_lo", "A", 8 * KB, [P, NG, SEQ], F32R)
    bT_hi = sb("bT_hi", "A", 16 * KB, [P, NH, SEQ], F32R)
    bT_lo = sb("bT_lo", "A", 24 * KB, [P, NH, SEQ], F32R)
    o_tok = sb("o_tok", "A", 0, [P, NT, D])
    f_tok = sb("f_tok", "A", 0, [P, NT, D])
    vg = sb("vg", "B", 0, [P, NT, SGW])
    uT = sb("uT", "B", 8 * KB, [P, NG, SEQ])
    vzT = sb("vzT", "B", 16 * KB, [P, NG, SEQ])
    ln_g = sb("ln_g", "B", 24 * KB, [P, SGW])
    ln_b = sb("ln_b", "B", 28 * KB, [P, SGW])
    sgb = sb("sgb", "B", 32 * KB, [P, NG, P])
    sgw = sb("sgw", "B", 36 * KB, [P, NG, P])
    v_tok = sb("v_tok", "B", 40 * KB, [P, NT, NKV * P])
    kT = sb("kT", "B", 42 * KB, [P, NKV, SEQ])
    mT_hi = sb("mT_hi", "B", 0, [P, KD, SEQ], F32R)
    mT_lo = sb("mT_lo", "B", 16 * KB, [P, KD, SEQ], F32R)
    g_ffn = sb("g_ffn", "B", 32 * KB, [P, D])
    act_hi = sb("act_hi", "B", 0, [P, HALF, SEQ], F32R)
    act_lo = sb("act_lo", "B", 22 * KB, [P, HALF, SEQ], F32R)
    gain = sb("gain", "gain", 0, [P, D])
    prob = [sb(f"prob{i}", "tmp", i * 2 * KB, [P, NT, SEQ]) for i in range(2)]
    pT = sb("pT", "tmp", 4 * KB, [P, NT, SEQ])
    qT = [sb(f"qT{i}", "tmp", (6 + i) * KB, [P, SEQ]) for i in range(2)]
    sig = [[sb(f"sig{p}{i}", "tmp", (2 * p + i) * KB, [P, SEQ]) for i in range(2)] for p in range(2)]
    squares = sb("squares", "tmp", 0, [P, BLK])
    conv_o = [[sb(f"conv_o{p}{i}", "tmp", (2 * p + i) * KB, [P, SEQ]) for i in range(2)] for p in range(2)]
    gelu_o = [sb(f"gelu_o{p}", "tmp", (4 + p) * KB, [P, SEQ]) for p in range(2)]
    prod = [sb(f"prod{p}", "tmp", (6 + p) * KB, [P, SEQ]) for p in range(2)]
    ident = sb("ident", "misc", 0, [P, P])
    convw = sb("convw", "misc", 512, [P, KF, 2, 4])
    small = sb("small", "misc", 512 + 1408, [P, 64])
    mask = sb("mask", "gain", 0, [P, NT, SEQ])
    ropes = sb("ropes", "gain", 2 * KB, [ROT, 2, SEQ])
    rot = sb("rot", "gain", 4 * KB, [ROT, SEQ])

    ssq, msq, rstd = small[:, 0:2], small[:, 2:4], small[:, 4:6]
    ssq4 = small[:, 6:14]
    neg_half = small[:, 14:15]
    mean_var = [small[:, 16 + 2 * t:18 + 2 * t] for t in range(NT)]
    stats = [small[:, 20 + 12 * t:32 + 12 * t] for t in range(NT)]
    smax, negm, psum_p, esink = (small[:, 44 + 2 * i:46 + 2 * i] for i in range(4))
    den, rden = small[:, 52:54], small[:, 54:56]
    sinks = small[:, 56:64]

    def one(tensor, n):
        return tensor[:, bass.ds(n, 1), :].rearrange("p o s -> p (o s)")

    bank = [nc.alloc_psum_tensor(f"bank{i}", [P, BLK], F32) for i in range(8)]

    def sem(name):
        return nc.alloc_semaphore(name)

    raw_ready = [sem(f"raw_ready{s}") for s in range(RING)]
    wh_ready, wl_ready, w_used = sem("wh_ready"), sem("wl_ready"), sem("w_used")
    x_in = [sem("x_in0"), sem("x_in1")]
    gain_in, misc_in, tables_in, sg_in = sem("gain_in"), sem("misc_in"), sem("tables_in"), sem("sg_in")
    post_in, ffn_gain_in, x_again, last_gain_in = sem("post_in"), sem("ffn_gain_in"), sem("x_again"), sem("last_gain_in")
    half_set = sem("half_set")
    sq_done, red_done, ms_done, rstd_done = (sem(n) for n in ("sq_done", "red_done", "ms_done", "rstd_done"))
    xn_done, tr_done, hh_done, hl_done = sem("xn_done"), sem("tr_done"), sem("hh_done"), sem("hl_done")
    vg_done, st_done, mv_done = sem("vg_done"), sem("st_done"), sem("mv_done")
    vhat_done, vmul_done, vn_done = sem("vhat_done"), sem("vmul_done"), sem("vn_done")
    vt_done = sem("vt_done")
    rope_copied, rope_turned, rope_sin, rope_cos, rope_done = (
        sem(n) for n in ("rope_copied", "rope_turned", "rope_sin", "rope_cos", "rope_done"))
    u_copied, vz_ready, vz_done = sem("u_copied"), sem("vz_ready"), sem("vz_done")
    sc_ready, sc_read, mx_done, nm_done, exp_done = (
        sem(n) for n in ("sc_ready", "sc_read", "mx_done", "nm_done", "exp_done"))
    den_done, rden_done, p_ready = sem("den_done"), sem("rden_done"), sem("p_ready")
    pt_ready, pt_free, pv_ready, bh_done, bl_free = (
        sem(n) for n in ("pt_ready", "pt_free", "pv_ready", "bh_done", "bl_free"))
    ug_done, a_done, ah_done, al_done = sem("ug_done"), sem("a_done"), sem("ah_done"), sem("al_done")
    sig_done, gated, m_done, mh_done, ml_done = (
        sem(n) for n in ("sig_done", "gated", "m_done", "mh_done", "ml_done"))
    o_ready, o_copied, o_sq = sem("o_ready"), sem("o_copied"), sem("o_sq")
    on_done, x1_done = sem("on_done"), sem("x1_done")
    c_mid, c_left, c_done, ge_done, pr_done, acth_done, act_done = (
        sem(n) for n in ("c_mid", "c_left", "c_done", "ge_done", "pr_done", "acth_done", "act_done"))
    f_done, f_sq, y_mul, y_done = sem("f_done"), sem("f_sq"), sem("y_mul"), sem("y_done")
    stored = sem("stored")

    N_PRE, N_V, N_POST, N_FFN, N_LAST = 0, 2, 4, 6, 8
    V_Q = RING * T_QU
    START_FREE = RING

    def load_unit(sp, T0, j, r=0):
        turn, slot = T0 + j // RING, j % RING
        if not exists(turn, slot):
            return
        if turn > 0:
            sp.wait_ge(wl_ready, (turn + r) * RING + slot - RING + 1)
        sp.dma_start(raw[slot][:, :], weights[(turn + r) * RING + slot - skipped(turn)]).then_inc(raw_ready[slot], 16)

    def round_unit(act, T0, j, r=0):
        turn, slot = T0 + j // RING, j % RING
        if not exists(turn, slot):
            return
        v = (turn + r) * RING + slot
        act.wait_ge(raw_ready[slot], (turn + r + 1 - (skipped(turn) if slot == RING - 1 else 0)) * 16)
        if turn > 0:
            act.wait_ge(w_used, v - RING + 1)
        act.activation(w_hi[slot][:, :], raw[slot][:, :], ACT.Copy).then_inc(wh_ready, counts_for(turn, slot))

    def rest_unit(dve, T0, j, r=0):
        turn, slot = T0 + j // RING, j % RING
        if not exists(turn, slot):
            return
        dve.wait_ge(wh_ready, (turn + r) * RING + slot + 1)
        dve.tensor_tensor(w_lo[slot][:, :], raw[slot][:, :], w_hi[slot][:, :], ALU.subtract).then_inc(
            wl_ready, counts_for(turn, slot))

    block = nc.Block()
    with block:
        @block.sync
        def _(sp):
            sp.dma_start(x_tok[:, 0, :], x[0]).then_inc(x_in[0], 16)
            sp.dma_start(gain[:, :], gains[0:1, :].partition_broadcast(P)).then_inc(gain_in, 16)
            sp.dma_start(ident[:, :], ident_in).then_inc(misc_in, 16)
            sp.dma_start(x_tok[:, 1, :], x[1]).then_inc(x_in[1], 16)
            for j in range(RING):
                load_unit(sp, 0, j)
            sp.dma_start(ln_g[:, :], sg_gb[0:1, :].partition_broadcast(P)).then_inc(sg_in, 16)
            sp.dma_start(ln_b[:, :], sg_gb[1:2, :].partition_broadcast(P)).then_inc(sg_in, 16)
            sp.dma_start(sgb[:, :, :], sg_b.partition_broadcast(P)).then_inc(sg_in, 16)
            sp.dma_start(sgw[:, :, :], sg_wT).then_inc(sg_in, 16)
            sp.dma_start(sinks, sink.partition_broadcast(P)).then_inc(sg_in, 16)
            sp.dma_start(convw[:, :, :, :], conv).then_inc(sg_in, 16)
            for j in range(RING):
                load_unit(sp, 1, j)
            sp.wait_ge(xn_done, NT)
            sp.dma_start(mask[:, :, :], mask_in).then_inc(tables_in, 16)
            sp.dma_start(ropes[:, :, :], rope_in).then_inc(tables_in, 16)
            with sp.Fori(0, T_MG + 1 - 2) as i:
                for j in range(RING):
                    load_unit(sp, 2, j, i)
            sp.wait_ge(sc_read, NH)
            sp.wait_ge(rope_done, NKV + NH)
            sp.dma_start(gain[:, :], gains[1:2, :].partition_broadcast(P)).then_inc(post_in, 16)
            with sp.Fori(0, T_OUT + 1 - (T_MG + 1)) as i:
                for j in range(RING):
                    load_unit(sp, T_MG + 1, j, i)
            sp.wait_ge(w_used, RING * T_OUT)
            for t in range(NT):
                sp.dma_start(x_tok[:, t, :], x[t]).then_inc(x_again, 16)
            sp.dma_start(g_ffn[:, :], gains[2:3, :].partition_broadcast(P)).then_inc(ffn_gain_in, 16)
            with sp.Fori(0, T_FFN - (T_OUT + 1)) as i:
                for j in range(RING):
                    load_unit(sp, T_OUT + 1, j, i)
            for h in range(2):
                T0 = T_FFN + h * HALF_TURNS
                with sp.Fori(0, UP_TURNS) as i:
                    for j in range(RING):
                        load_unit(sp, T0, j, i)
                if h == 0:
                    sp.wait_ge(on_done, NT)
                    sp.dma_start(gain[:, :], gains[3:4, :].partition_broadcast(P)).then_inc(last_gain_in, 16)
                for n in range(2):
                    for j in range(DOWN_TURNS * RING):
                        load_unit(sp, T0 + UP_TURNS + n * DOWN_TURNS, j)
            for t in range(NT):
                sp.wait_ge(y_done, t + 1)
                sp.dma_start(out[t], f_tok[:, t, :]).then_inc(stored, 16)
            sp.wait_ge(stored, 16 * NT)

        @block.gpsimd
        def _(pool):
            pool.memset(neg_half, -0.5).then_inc(half_set, 1)
            pool.wait_ge(half_set, 1)

            def power(n, t):
                pool.wait_ge(ms_done, n + t + 1)
                pool.tensor_tensor(rstd[:, t:t + 1], msq[:, t:t + 1], neg_half, ALU.pow).then_inc(rstd_done, 1)

            def rope(n, dst, ahead=0):
                c = n + 1 + ahead
                pool.wait_ge(rope_turned, c)
                pool.tensor_tensor(rot[:, :], rot[:, :], ropes[:, 1, :], ALU.mult).then_inc(rope_sin, 1)
                pool.tensor_tensor(dst, dst, ropes[:, 0, :], ALU.mult).then_inc(rope_cos, 1)
                pool.wait_ge(rope_sin, c)
                pool.wait_ge(rope_cos, c)
                pool.tensor_tensor(dst, dst, rot[:, :], ALU.add).then_inc(rope_done, 1)

            for t in range(NT):
                power(N_PRE, t)
            pool.wait_ge(sg_in, 16 * 6)
            for t in range(NT):
                power(N_V, t)
                pool.wait_ge(vhat_done, t + 1)
                pool.tensor_tensor(vg[:, t, :], vg[:, t, :], ln_g[:, :], ALU.mult).then_inc(vmul_done, 1)
                pool.wait_ge(vmul_done, t + 1)
                pool.tensor_tensor(vg[:, t, :], vg[:, t, :], ln_b[:, :], ALU.add).then_inc(vn_done, 1)
            pool.wait_ge(tables_in, 32)
            for g in range(NKV):
                rope(g, kT[0:ROT, g, :])
            with pool.Fori(0, NH // 2) as i:
                for p in range(2):
                    rope(NKV + p, qT[p][0:ROT, :], 2 * i)
            for n in (N_POST, N_FFN):
                for t in range(NT):
                    power(n, t)
            for t in range(NT):
                power(N_LAST, t)

        @block.scalar
        def _(act):
            def square(n, t, src, junk):
                act.activation(junk, src, ACT.Square, accum_out=ssq[:, t:t + 1]).then_inc(sq_done, 1)

            def turn_hi(first_bank, n, t):
                for b in range(NB):
                    act.wait_ge(tr_done, n + NB * t + b + 1)
                    act.activation(hT_hi[:, 4 * b:4 * b + 4, t * P:(t + 1) * P],
                                   bank[first_bank + b][:, :].rearrange("p (k s) -> p k s", k=4),
                                   ACT.Copy).then_inc(hh_done, 1)

            def rope_copy(v, b, dst, n):
                act.wait_ge(w_used, v + 1)
                act.activation(dst, bank[b][:, 0:SEQ], ACT.Copy).then_inc(rope_copied, 1)

            def exps(h, p):
                act.wait_ge(nm_done, h + 1)
                for t in range(NT):
                    act.activation(prob[p][:, t, :], prob[p][:, t, :], ACT.Exp, bias=negm[:, t:t + 1],
                                   accum_out=psum_p[:, t:t + 1]).then_inc(exp_done, 1)
                act.activation(esink, negm, ACT.Exp, bias=sinks[:, bass.ds(h, 1)]).then_inc(exp_done, 1)

            def b_hi(h):
                act.wait_ge(pv_ready, h + 1)
                act.activation(one(bT_hi, h), bank[6][:, 0:SEQ], ACT.Copy).then_inc(bh_done, 1)

            def head(h, p, T0, r, first=False, second=False):
                q = V_Q + 2 * h
                round_unit(act, T0, 2 * p + 3, r)
                if not (first or second):
                    act.wait_ge(sc_ready, h - 1)
                rope_copy(q, p, qT[p][:, :], h)
                if not first:
                    exps(h - 1, 1 - p)
                round_unit(act, T0, 2 * p + 4, r)
                act.wait_ge(w_used, q + 2)
                act.activation(one(uT, h), bank[2 + p][:, 0:SEQ], ACT.Copy).then_inc(u_copied, 1)
                if not (first or second):
                    b_hi(h - 2)

            for j in range(RING - 1):
                if j == 1:
                    act.wait_ge(x_in[0], 16)
                    square(N_PRE, 0, x_tok[:, 0, :], xn[:, 0, :])
                    act.wait_ge(x_in[1], 16)
                    square(N_PRE, 1, x_tok[:, 1, :], xn[:, 1, :])
                round_unit(act, 0, j)
            turn_hi(0, 0, 0)
            turn_hi(4, 0, 1)
            for b in range(2):
                for j in range(RING):
                    round_unit(act, b, j + 3)
                act.wait_ge(w_used, RING * (b + 1))
                for t in range(NT):
                    act.activation(vg[:, t, b * BLK:(b + 1) * BLK], bank[2 * b + t][:, :], ACT.Gelu_apprx_tanh).then_inc(vg_done, 1)
            round_unit(act, T_KV, 3)
            round_unit(act, T_KV, 4)
            act.wait_ge(w_used, RING * T_KV + 2)
            for t in range(NT):
                act.activation(v_tok[:, t, :], bank[4 + t][:, 0:SEQ], ACT.Copy).then_inc(vt_done, 1)
            for g in range(NKV):
                round_unit(act, T_KV, 5 + g)
                rope_copy(RING * T_KV + 2 + g, 6 + g, kT[:, g, :], g)
            act.wait_ge(sg_in, 16 * 6)
            head(0, 0, T_QU, 0, first=True)
            head(1, 1, T_QU, 0, second=True)
            with act.Fori(1, NH // 2) as i:
                for p in range(2):
                    head(2 * i + p, p, T_QU, i)

            def sigmoid(n, i, p, v, guard=True):
                act.wait_ge(w_used, v + 1)
                if guard:
                    act.wait_ge(ml_done, n - 1)
                act.activation(sig[p][i][:, :], bank[2 * p + i][:, 0:SEQ], ACT.Sigmoid).then_inc(sig_done, 1)

            def m_hi(n, p):
                act.wait_ge(m_done, n + 1)
                act.activation(one(mT_hi, n), sig[p][0][:, :], ACT.Copy).then_inc(mh_done, 1)

            def pair(T0, j0, r, n, first=False):
                v = (T0 + r) * RING + j0
                if first:
                    round_unit(act, T0, j0 + 3, r)
                    exps(NH - 1, 1)
                    b_hi(NH - 2)
                    round_unit(act, T0, j0 + 4, r)
                    b_hi(NH - 1)
                    act.wait_ge(u_copied, NG)
                    act.activation(uT[:, :, :], uT[:, :, :], ACT.Gelu_apprx_tanh).then_inc(ug_done, 1)
                    act.wait_ge(a_done, 1)
                    act.activation(aT_hi[:, :, :], uT[:, :, :], ACT.Copy).then_inc(ah_done, 1)
                    for g in range(4):
                        if g > 1:
                            round_unit(act, T0, j0 + 3 + g, r)
                        if g == 0:
                            act.wait_ge(pv_ready, NH)
                            act.wait_ge(bh_done, NH)
                        sigmoid(n + g // 2, g % 2, g // 2, v + g, guard=False)
                else:
                    for g in range(4):
                        round_unit(act, T0, j0 + 3 + g, r)
                        sigmoid(n + g // 2, g % 2, g // 2, v + g)
                for p in range(2):
                    round_unit(act, T0, j0 + 7 + p, r)
                    m_hi(n + p, p)

            pair(T_MG, 0, 0, 0, first=True)
            pair(T_MG, 6, 0, 2)
            with act.Fori(1, KD // 4) as i:
                pair(T_MG, 0, 3 * i, 4 * i)
                pair(T_MG, 6, 3 * i, 4 * i + 2)

            for b in range(NB):
                round_unit(act, T_OUT + b, 3)
                for t in range(NT):
                    if t == 1:
                        round_unit(act, T_OUT + b, 4)
                        round_unit(act, T_OUT + b, 5)
                    act.wait_ge(o_copied, 2 * b + t + 1)
                    if b + t > 0:
                        act.wait_ge(o_sq, 2 * b + t)
                    act.activation(squares[:, :], o_tok[:, t, b * BLK:(b + 1) * BLK], ACT.Square,
                                   accum_out=ssq4[:, NB * t + b:NB * t + b + 1]).then_inc(o_sq, 1)
                round_unit(act, T_OUT + b, 6)
            for t in range(NT):
                act.wait_ge(x1_done, t + 1)
                square(N_FFN, t, x_tok[:, t, :], o_tok[:, t, :])
            turn_hi(4, NB * NT, 0)
            turn_hi(0, NB * NT, 1)

            act.wait_ge(o_sq, NB * NT)

            def up(T0, j0, r, pp, h):
                p = (j0 // 2) % 2
                v = (T0 + r) * RING + j0
                for i in range(2):
                    round_unit(act, T0, j0 + i + 3, r)
                    act.wait_ge(w_used, v + i + 1)
                    act.wait_ge(pr_done, pp + 1)
                    act.activation(conv_o[p][i][:, :], bank[2 * p + i][:, 0:SEQ], ACT.Identity,
                                   scale=convw[:, bass.ds(pp, 1), i, 1], bias=convw[:, bass.ds(pp, 1), i, 3]).then_inc(c_mid, 1)
                act.wait_ge(c_done, START_FREE + 2 * pp + 1)
                act.activation(gelu_o[p][:, :], conv_o[p][0][:, :], ACT.Gelu_apprx_tanh).then_inc(ge_done, 1)
                act.wait_ge(pr_done, pp + 1 + 2)
                act.activation(one(act_hi, pp - HALF * h), prod[p][:, :], ACT.Copy).then_inc(acth_done, 1)

            for h in range(2):
                T0 = T_FFN + h * HALF_TURNS
                with act.Fori(0, UP_TURNS) as i:
                    for q in range(2):
                        up(T0, 2 * q, i, 2 * i + q + HALF * h, h)
                for n in range(2):
                    for j in range(DOWN_TURNS * RING):
                        round_unit(act, T0 + UP_TURNS + n * DOWN_TURNS, j + 3)
            for n in range(2):
                for t in range(NT):
                    for c in range(2):
                        b = 2 * n + c
                        act.wait_ge(f_done, 8 + 4 * n + 2 * t + c + 1)
                        if n + t + c > 0:
                            act.wait_ge(f_sq, 4 * n + 2 * t + c)
                        act.activation(squares[:, :], f_tok[:, t, b * BLK:(b + 1) * BLK], ACT.Square,
                                       accum_out=ssq4[:, NB * t + b:NB * t + b + 1]).then_inc(f_sq, 1)

        @block.vector
        def _(dve):
            def mean_square(t):
                dve.tensor_scalar(msq[:, t:t + 1], ssq[:, t:t + 1], 1.0 / D, EPS, ALU.mult, ALU.add).then_inc(ms_done, 1)

            def mean_square4(t, count):
                dve.tensor_reduce(ssq[:, t:t + 1], ssq4[:, NB * t:NB * t + NB], AX.X, ALU.add).then_inc(red_done, 1)
                dve.wait_ge(red_done, count)
                mean_square(t)

            def normalise(dst, src, t, g, n, done):
                dve.wait_ge(rstd_done, n + t + 1)
                return dve.scalar_tensor_tensor(dst, src, rstd[:, t:t + 1], g, ALU.mult, ALU.mult).then_inc(done, 1)

            def turn_lo(first_bank, n, t):
                for b in range(NB):
                    dst = (slice(None), slice(4 * b, 4 * b + 4), slice(t * P, (t + 1) * P))
                    dve.wait_ge(hh_done, n + NB * t + b + 1)
                    dve.tensor_tensor(hT_lo[dst], bank[first_bank + b][:, :].rearrange("p (k s) -> p k s", k=4),
                                      hT_hi[dst], ALU.subtract).then_inc(hl_done, 1)

            def turned(n, src):
                dve.wait_ge(rope_copied, n + 1)
                if not isinstance(n, int) or n > 0:
                    dve.wait_ge(rope_done, n)
                dve.stream_shuffle(rot[:, :], src, [(i + ROT // 2) % ROT for i in range(ROT)]).then_inc(rope_turned, 1)

            def scores(h, p, guard=True):
                dve.wait_ge(sc_ready, h + 1)
                if guard:
                    dve.wait_ge(pt_ready, h - 1)
                dve.scalar_tensor_tensor(prob[p][:, :, :], bank[4][:, :].rearrange("p (t s) -> p t s", t=NT), SCALE,
                                         mask[:, :, :], ALU.mult, ALU.add).then_inc(sc_read, 1)
                dve.wait_ge(sc_read, h + 1)
                dve.tensor_reduce(smax, prob[p][:, :, :], AX.X, ALU.max).then_inc(mx_done, 1)
                dve.wait_ge(mx_done, h + 1)
                dve.tensor_scalar(negm, smax, sinks[:, bass.ds(h, 1)], -1.0, ALU.max, ALU.mult).then_inc(nm_done, 1)

            def probabilities(h, p):
                dve.wait_ge(exp_done, 3 * h + 3)
                dve.tensor_tensor(den, psum_p, esink, ALU.add).then_inc(den_done, 1)
                dve.wait_ge(den_done, h + 1)
                dve.reciprocal(rden, den).then_inc(rden_done, 1)
                dve.wait_ge(rden_done, h + 1)
                for t in range(NT):
                    dve.tensor_scalar(prob[p][:, t, :], prob[p][:, t, :], rden[:, t:t + 1], None, ALU.mult).then_inc(p_ready, 1)

            def copy_pT(h, guard=True):
                dve.wait_ge(pt_ready, h + 1)
                if guard:
                    dve.wait_ge(pv_ready, h)
                dve.tensor_copy(pT[:, :, :], bank[5][:, :].rearrange("p (k s) -> p k s", k=NT)).then_inc(pt_free, 1)

            def vz(h):
                dve.wait_ge(vz_ready, h + 1)
                dve.tensor_tensor(vzT[:, bass.ds(h, 1), :].rearrange("p g (c t) -> p (g c) t", c=NT),
                                  bank[7][:, 0:SEQ].rearrange("p (c t) -> p c t", c=NT),
                                  sgb[:, bass.ds(h, 1), :].broadcast_to([P, NT, P]), ALU.add).then_inc(vz_done, 1)

            def b_lo(h):
                dve.wait_ge(bh_done, h + 1)
                dve.tensor_tensor(one(bT_lo, h), bank[6][:, 0:SEQ], one(bT_hi, h), ALU.subtract).then_inc(bl_free, 1)

            def head(h, p, T0, r, first=False, second=False, third=False):
                rest_unit(dve, T0, 2 * p + 3, r)
                turned(NKV + h, qT[p][0:ROT, :])
                if not first:
                    scores(h - 1, 1 - p, guard=not (second or third))
                rest_unit(dve, T0, 2 * p + 4, r)
                if not first:
                    probabilities(h - 1, 1 - p)
                if not (first or second):
                    copy_pT(h - 2, guard=not third)
                vz(h)
                if not (first or second):
                    b_lo(h - 2)

            for t in range(NT):
                dve.wait_ge(sq_done, t + 1)
                mean_square(t)
                if t == 0:
                    dve.wait_ge(gain_in, 16)
                normalise(xn[:, t, :], x_tok[:, t, :], t, gain[:, :], N_PRE, xn_done)
                rest_unit(dve, 0, t)
            turn_lo(0, 0, 0)
            turn_lo(4, 0, 1)
            rest_unit(dve, 0, 2)
            for b in range(2):
                for j in range(RING):
                    rest_unit(dve, b, j + 3)
                for t in range(NT):
                    dve.wait_ge(vg_done, NT * b + t + 1)
                    dve.bn_stats(stats[t][:, 6 * b:6 * b + 6], vg[:, t, b * BLK:(b + 1) * BLK]).then_inc(st_done, 1)
            rest_unit(dve, T_KV, 3)
            for t in range(NT):
                dve.wait_ge(st_done, 3 + t)
                dve.bn_aggr(mean_var[t], stats[t]).then_inc(mv_done, 1)
                dve.wait_ge(mv_done, t + 1)
                dve.tensor_scalar(msq[:, t:t + 1], mean_var[t][:, 1:2], EPS, None, ALU.add).then_inc(ms_done, 1)
            for t in range(NT):
                dve.wait_ge(rstd_done, N_V + t + 1)
                dve.tensor_scalar(vg[:, t, :], vg[:, t, :], mean_var[t][:, 0:1], rstd[:, t:t + 1],
                                  ALU.subtract, ALU.mult).then_inc(vhat_done, 1)
            rest_unit(dve, T_KV, 4)
            for g in range(NKV):
                rest_unit(dve, T_KV, 5 + g)
                turned(g, kT[0:ROT, g, :])
            dve.wait_ge(tables_in, 32)
            dve.wait_ge(sg_in, 16 * 6)
            dve.sem_inc(pt_free, 1)
            dve.sem_inc(bl_free, 1)
            for h in range(NH):
                head(h, h % 2, T_QU + h // 2, 0, first=h == 0, second=h == 1, third=h == 2)

            def merged(n, p):
                for i in range(2):
                    dve.tensor_tensor(sig[p][i][:, :], sig[p][i][:, :], bank[4 + 2 * p + i][:, 0:SEQ], ALU.mult).then_inc(gated, 1)
                dve.wait_ge(gated, 2 * n + 2)
                dve.tensor_tensor(sig[p][0][:, :], sig[p][0][:, :], sig[p][1][:, :], ALU.add).then_inc(m_done, 1)
                dve.wait_ge(mh_done, n + 1)
                dve.tensor_tensor(one(mT_lo, n), sig[p][0][:, :], one(mT_hi, n), ALU.subtract).then_inc(ml_done, 1)

            def pair(T0, j0, r, n, first=False):
                v = (T0 + r) * RING + j0
                if first:
                    rest_unit(dve, T0, j0 + 3, r)
                    scores(NH - 1, 1)
                    copy_pT(NH - 2)
                    rest_unit(dve, T0, j0 + 4, r)
                    b_lo(NH - 2)
                    probabilities(NH - 1, 1)
                    copy_pT(NH - 1)
                    b_lo(NH - 1)
                    dve.wait_ge(ug_done, 1)
                    dve.wait_ge(vz_done, NG)
                    dve.tensor_tensor(uT[:, :, :], uT[:, :, :], vzT[:, :, :], ALU.mult).then_inc(a_done, 1)
                    dve.wait_ge(ah_done, 1)
                    dve.tensor_tensor(aT_lo[:, :, :], uT[:, :, :], aT_hi[:, :, :], ALU.subtract).then_inc(al_done, 1)
                    for g in range(2, 4):
                        rest_unit(dve, T0, j0 + 3 + g, r)
                else:
                    for g in range(4):
                        rest_unit(dve, T0, j0 + 3 + g, r)
                for p in range(2):
                    rest_unit(dve, T0, j0 + 7 + p, r)
                    dve.wait_ge(sig_done, 2 * (n + p) + 2)
                    dve.wait_ge(w_used, v + 4 + p + 1)
                    merged(n + p, p)

            pair(T_MG, 0, 0, 0, first=True)
            pair(T_MG, 6, 0, 2)
            with dve.Fori(1, KD // 4) as i:
                pair(T_MG, 0, 3 * i, 4 * i)
                pair(T_MG, 6, 3 * i, 4 * i + 2)

            for b in range(NB):
                rest_unit(dve, T_OUT + b, 3)
                for t in range(NT):
                    if t == 0:
                        dve.wait_ge(o_ready, b + 1)
                    else:
                        rest_unit(dve, T_OUT + b, 4)
                        rest_unit(dve, T_OUT + b, 5)
                        dve.wait_ge(w_used, RING * (T_OUT + b + 1))
                    dve.tensor_copy(o_tok[:, t, b * BLK:(b + 1) * BLK], bank[2 * (b % 2) + t][:, :]).then_inc(o_copied, 1)
                    if b == NB - 1:
                        dve.wait_ge(o_sq, 2 * b + t + 1)
                        mean_square4(t, t + 1)
                        dve.wait_ge(post_in, 16)
                        dve.wait_ge(x_again, 16 * NT)
                        dve.wait_ge(o_copied, 2 * b + t + 1)
                        normalise(o_tok[:, t, :], o_tok[:, t, :], t, gain[:, :], N_POST, on_done)
                        dve.wait_ge(on_done, t + 1)
                        dve.tensor_tensor(x_tok[:, t, :], x_tok[:, t, :], o_tok[:, t, :], ALU.add).then_inc(x1_done, 1)
                if b < NB - 1:
                    rest_unit(dve, T_OUT + b, 6)
            dve.wait_ge(ffn_gain_in, 16)
            for t in range(NT):
                dve.wait_ge(sq_done, NT + t + 1)
                mean_square(t)
                normalise(o_tok[:, t, :], x_tok[:, t, :], t, g_ffn[:, :], N_FFN, xn_done)
            turn_lo(4, NB * NT, 0)
            rest_unit(dve, T_OUT + NB - 1, 6)
            turn_lo(0, NB * NT, 1)

            dve.sem_inc(c_done, START_FREE)
            dve.sem_inc(pr_done, 2)

            def up(T0, j0, r, pp, h):
                p = (j0 // 2) % 2
                for i in range(2):
                    c = conv_o[p][i]
                    src = bank[2 * p + i]
                    rest_unit(dve, T0, j0 + i + 3, r)
                    dve.wait_ge(c_mid, 2 * pp + i + 1)
                    dve.scalar_tensor_tensor(c[:, 1:SEQ], src[:, 0:SEQ - 1], convw[:, bass.ds(pp, 1), i, 0], c[:, 1:SEQ],
                                             ALU.mult, ALU.add).then_inc(c_left, 1)
                    dve.wait_ge(c_left, 2 * pp + i + 1)
                    dve.scalar_tensor_tensor(c[:, 0:SEQ - 1], src[:, 1:SEQ], convw[:, bass.ds(pp, 1), i, 2], c[:, 0:SEQ - 1],
                                             ALU.mult, ALU.add).then_inc(c_done, 1)
                dve.wait_ge(ge_done, pp + 1)
                dve.wait_ge(c_done, START_FREE + 2 * pp + 2)
                dve.tensor_tensor(prod[p][:, :], gelu_o[p][:, :], conv_o[p][1][:, :], ALU.mult).then_inc(pr_done, 1)
                dve.wait_ge(acth_done, pp + 1)
                dve.tensor_tensor(one(act_lo, pp - HALF * h), prod[p][:, :], one(act_hi, pp - HALF * h),
                                  ALU.subtract).then_inc(act_done, 1)

            def f_block(h, n):
                for t in range(NT):
                    for c in range(2):
                        k = 4 * n + 2 * t + c
                        col = slice((2 * n + c) * BLK, (2 * n + c + 1) * BLK)
                        src = bank[4 * (1 - n) + 2 * t + c]
                        dve.wait_ge(w_used, RING * (T_FFN + h * HALF_TURNS + UP_TURNS + (n + 1) * DOWN_TURNS))
                        if h == 0:
                            dve.tensor_copy(f_tok[:, t, col], src[:, :]).then_inc(f_done, 1)
                        else:
                            dve.wait_ge(f_done, k + 1)
                            dve.tensor_tensor(f_tok[:, t, col], f_tok[:, t, col], src[:, :], ALU.add).then_inc(f_done, 1)

            for h in range(2):
                T0 = T_FFN + h * HALF_TURNS
                with dve.Fori(0, UP_TURNS) as i:
                    for q in range(2):
                        up(T0, 2 * q, i, 2 * i + q + HALF * h, h)
                for n in range(2):
                    for j in range(DOWN_TURNS * RING):
                        rest_unit(dve, T0 + UP_TURNS + n * DOWN_TURNS, j + 3)
                        if j == 0 and n == 1:
                            f_block(h, 0)
                f_block(h, 1)
            dve.wait_ge(last_gain_in, 16)
            for t in range(NT):
                dve.wait_ge(f_sq, 6 + 2 * t)
                mean_square4(t, NT + t + 1)
                dve.wait_ge(f_done, 14 + 2 * t)
                normalise(f_tok[:, t, :], f_tok[:, t, :], t, gain[:, :], N_LAST, y_mul)
                dve.wait_ge(y_mul, t + 1)
                dve.tensor_tensor(f_tok[:, t, :], f_tok[:, t, :], x_tok[:, t, :], ALU.add).then_inc(y_done, 1)

        @block.tensor
        def _(pe):
            def passes(dst, a_hi, a_lo, b_hi, b_lo, first, last):
                pe.matmul(dst, a_hi, b_hi, start=first, stop=False)
                pe.matmul(dst, a_hi, b_lo, start=False, stop=False)
                return pe.matmul(dst, a_lo, b_hi, start=False, stop=last)

            def arrived(T0, j, r=0):
                pe.wait_ge(wl_ready, (T0 + r) * RING + j + 1)

            def stationary(T0, j, r, dst, rhs_hi, rhs_lo, ks=range(KD), done=None):
                hi = w_hi[j % RING][:, :].rearrange("p (k m) -> p k m", m=P)
                lo = w_lo[j % RING][:, :].rearrange("p (k m) -> p k m", m=P)
                for k in ks:
                    i = k - ks[0]
                    last = passes(dst, hi[:, k, :], lo[:, k, :], rhs_hi[:, i, :], rhs_lo[:, i, :], i == 0, i == len(ks) - 1)
                if done is None:
                    last.then_inc(w_used, 1)

            def tokens(T0, b, banks, src_hi, src_lo, waits=None, ready=None):
                for t in range(NT):
                    for c in range(RING):
                        if t == 0:
                            arrived(T0, c)
                        if waits:
                            waits(t, c)
                        hi = w_hi[c][:, :].rearrange("p (k n) -> p k n", n=BLK)
                        lo = w_lo[c][:, :].rearrange("p (k n) -> p k n", n=BLK)
                        for kk in range(4):
                            k = 4 * c + kk
                            tt = slice(t * P, (t + 1) * P)
                            dst = banks[t][:, :]
                            pe.matmul(dst, src_hi[:, k, tt], hi[:, kk, :], start=k == 0, stop=False)
                            pe.matmul(dst, src_hi[:, k, tt], lo[:, kk, :], start=False, stop=False)
                            last = pe.matmul(dst, src_lo[:, k, tt], hi[:, kk, :], start=False, stop=k == KD - 1)
                        if t == NT - 1:
                            last.then_inc(w_used, 1)
                        elif ready is not None and c == RING - 1:
                            last.then_inc(ready, 1)

            def turn_tile(src, first_bank, n, t):
                pe.wait_ge(xn_done, n + t + 1)
                for b in range(NB):
                    for k in range(4):
                        last = pe.transpose(bank[first_bank + b][:, k * P:(k + 1) * P],
                                            src[:, t, (4 * b + k) * P:(4 * b + k + 1) * P], ident[:, :])
                    last.then_inc(tr_done, 1)

            def scores(h, p, guard=True):
                pe.wait_ge(rope_done, NKV + h + 1)
                if guard:
                    pe.wait_ge(sc_read, h)
                g = kv_of(h, p)
                for t in range(NT):
                    last = pe.matmul(bank[4][:, t * SEQ:(t + 1) * SEQ], qT[p][:, t * P:(t + 1) * P], g, start=True, stop=True)
                last.then_inc(sc_ready, 1)

            def kv_of(h, p):
                return kT[:, bass.ds(h // QPK, 1), :].rearrange("p g s -> p (g s)")

            def turn_probs(h, p):
                pe.wait_ge(p_ready, 2 * h + 2)
                pe.wait_ge(pt_free, h + 1)
                for t in range(NT):
                    for k in range(NT):
                        last = pe.transpose(bank[5][:, k * SEQ + t * P:k * SEQ + (t + 1) * P],
                                            prob[p][:, t, k * P:(k + 1) * P], ident[:, :])
                last.then_inc(pt_ready, 1)

            def values(h, g):
                pe.wait_ge(pt_free, h + 2)
                pe.wait_ge(bl_free, h + 1)
                for k in range(NT):
                    last = pe.matmul(bank[6][:, 0:SEQ], v_tok[:, k, g * P:(g + 1) * P], pT[:, k, :],
                                     start=k == 0, stop=k == NT - 1)
                last.then_inc(pv_ready, 1)

            def spatial(h, guard=True):
                if guard:
                    pe.wait_ge(vz_done, h)
                for c in range(NT):
                    last = pe.matmul(bank[7][:, c * P:(c + 1) * P], vg[:, c, h * P:(h + 1) * P], sgw[:, h, :],
                                     start=True, stop=True)
                last.then_inc(vz_ready, 1)

            def head(h, T0):
                p = h % 2
                r = h // 2
                arrived(T0, 2 * p, r)
                if h >= 2:
                    pe.wait_ge(rope_copied, NKV + h - 1)
                stationary(T0, 2 * p, r, bank[p][:, 0:SEQ], hT_hi, hT_lo)
                if h >= 1:
                    scores(h - 1, 1 - p, guard=h >= 2)
                if h >= 2:
                    turn_probs(h - 2, p)
                arrived(T0, 2 * p + 1, r)
                if h >= 2:
                    pe.wait_ge(u_copied, h - 1)
                stationary(T0, 2 * p + 1, r, bank[2 + p][:, 0:SEQ], hT_hi, hT_lo)
                if h == 0:
                    pe.wait_ge(vn_done, NT)
                    pe.wait_ge(sg_in, 16 * 6)
                spatial(h, guard=h >= 1)
                if h >= 2:
                    values(h - 2, (h - 2) // QPK)

            pe.wait_ge(misc_in, 16)
            turn_tile(xn, 0, 0, 0)
            turn_tile(xn, 4, 0, 1)

            def v_waits(t, c):
                if c == 0:
                    pe.wait_ge(hl_done, NB * (t + 1))
            tokens(0, 0, bank[0:2], hT_hi, hT_lo, waits=v_waits)
            tokens(1, 1, bank[2:4], hT_hi, hT_lo)
            for c in range(2):
                arrived(T_KV, c)
                hi = w_hi[c][:, :].rearrange("p (k n) -> p k n", n=SEQ)
                lo = w_lo[c][:, :].rearrange("p (k n) -> p k n", n=SEQ)
                for kk in range(8):
                    k = 8 * c + kk
                    for t in range(NT):
                        tt = slice(t * P, (t + 1) * P)
                        last = passes(bank[4 + t][:, 0:SEQ], hT_hi[:, k, tt], hT_lo[:, k, tt], hi[:, kk, :], lo[:, kk, :],
                                      k == 0, k == KD - 1)
                last.then_inc(w_used, 1)
            for g in range(NKV):
                arrived(T_KV, 2 + g)
                stationary(T_KV, 2 + g, 0, bank[6 + g][:, 0:SEQ], hT_hi, hT_lo)
            pe.wait_ge(vg_done, 2 * NT)
            pe.wait_ge(vt_done, NT)
            pe.wait_ge(rope_copied, NKV)
            for h in range(NH):
                head(h, T_QU)

            def branches(T0, j, r, p, guard):
                arrived(T0, j, r)
                if guard is not None:
                    pe.wait_ge(gated, guard)
                stationary(T0, j, r, bank[4 + 2 * p][:, 0:SEQ], aT_hi, aT_lo, ks=range(0, 8), done=False)
                stationary(T0, j, r, bank[5 + 2 * p][:, 0:SEQ], bT_hi, bT_lo, ks=range(8, 16))

            def pair(T0, j0, r, n, first=False):
                for g in range(4):
                    arrived(T0, j0 + g, r)
                    if not first:
                        pe.wait_ge(sig_done, 2 * n + g - 3)
                    else:
                        if g == 0:
                            pe.wait_ge(rope_copied, NKV + NH)
                            pe.wait_ge(u_copied, NG)
                    stationary(T0, j0 + g, r, bank[g][:, 0:SEQ], hT_hi, hT_lo)
                    if first and g == 0:
                        scores(NH - 1, 1)
                        turn_probs(NH - 2, 0)
                        values(NH - 2, 1)
                    if first and g == 1:
                        turn_probs(NH - 1, 1)
                        values(NH - 1, 1)
                if first:
                    pe.wait_ge(bl_free, NH + 1)
                    pe.wait_ge(al_done, 1)
                for p in range(2):
                    branches(T0, j0 + 4 + p, r, p, None if first else 2 * (n + p) - 2)

            pair(T_MG, 0, 0, 0, first=True)
            pair(T_MG, 6, 0, 2)
            with pe.Fori(1, KD // 4) as i:
                pair(T_MG, 0, 3 * i, 4 * i)
                pair(T_MG, 6, 3 * i, 4 * i + 2)

            for b in range(NB):
                def o_waits(t, c):
                    if b == 0 and t == 0:
                        if c == 0:
                            pe.wait_ge(sig_done, 2 * KD)
                        pe.wait_ge(ml_done, 4 * c + 4)
                    if b >= 2 and c == 0:
                        pe.wait_ge(o_copied, 2 * (b - 2) + t + 1)
                tokens(T_OUT + b, b, bank[2 * (b % 2):2 * (b % 2) + 2], mT_hi, mT_lo, waits=o_waits, ready=o_ready)
            turn_tile(o_tok, 4, NT, 0)
            pe.wait_ge(o_copied, 2 * NB)
            turn_tile(o_tok, 0, NT, 1)
            pe.wait_ge(hl_done, 2 * NB * NT)

            for h in range(2):
                T0 = T_FFN + h * HALF_TURNS
                if h == 1:
                    pe.wait_ge(f_done, 8)
                with pe.Fori(0, UP_TURNS) as i:
                    for j in range(RING):
                        arrived(T0, j, i)
                        pe.wait_ge(c_done, (i + UP_TURNS * h) * RING + j + 1)
                        stationary(T0, j, i, bank[j][:, 0:SEQ], hT_hi, hT_lo)
                for n in range(2):
                    T1 = T0 + UP_TURNS + n * DOWN_TURNS
                    first_bank = 4 * (1 - n)
                    if n == 0 and h == 1:
                        pe.wait_ge(f_done, 4)
                    if n == 1:
                        pe.wait_ge(c_done, START_FREE + 2 * HALF * (h + 1))
                    for j in range(DOWN_UNITS):
                        slot = j % RING
                        arrived(T1, j)
                        pe.wait_ge(act_done, HALF * h + 2 * j + 2)
                        hi = w_hi[slot][:, :].rearrange("p (k c n) -> p k c n", k=2, c=2)
                        lo = w_lo[slot][:, :].rearrange("p (k c n) -> p k c n", k=2, c=2)
                        for kk in range(2):
                            k = 2 * j + kk
                            first, final = k == 0, k == HALF - 1
                            for t in range(NT):
                                tt = slice(t * P, (t + 1) * P)
                                dst = [bank[first_bank + 2 * t + c][:, :] for c in range(2)]
                                for c in range(2):
                                    pe.matmul(dst[c], act_hi[:, k, tt], hi[:, kk, c, :], start=first, stop=False)
                                for c in range(2):
                                    pe.matmul(dst[c], act_hi[:, k, tt], lo[:, kk, c, :], start=False, stop=False)
                                for c in range(2):
                                    last = pe.matmul(dst[c], act_lo[:, k, tt], hi[:, kk, c, :], start=False, stop=final)
                        last.then_inc(w_used, counts_for(T1 + j // RING, slot))


def _constants():
    import numpy as np
    ident = np.eye(P, dtype=np.float32)
    q = np.arange(P)[:, None, None] + P * np.arange(NT)[None, :, None]
    k = np.arange(SEQ)[None, None, :]
    mask = np.where(np.abs(k - q) <= P, 0.0, MASK_VALUE).astype(np.float32)
    pos = np.arange(SEQ, dtype=np.float32)
    inv = np.float32(ROPE_THETA) ** (-np.arange(0, ROT, 2, dtype=np.float32) / np.float32(ROT))
    ang = (pos[None, :] * inv[:, None]).astype(np.float32)
    cos, sin = np.cos(ang).astype(np.float32), np.sin(ang).astype(np.float32)
    rope = np.stack([np.concatenate([cos, cos]), np.concatenate([-sin, sin])], axis=1)
    return ident, mask, np.ascontiguousarray(rope)


def _pack(w_in, w_a, w_b, w_out, w_up, w_down):
    import numpy as np
    units = []

    def rows(w, k0, nk, c0, nc_):
        return w[k0 * P:(k0 + nk) * P, c0:c0 + nc_].reshape(nk, P, nc_).transpose(1, 0, 2)

    def add(*parts):
        units.append(np.concatenate([p.reshape(P, -1) for p in parts], axis=1))

    u0, v0, q0 = 0, SGW, 2 * SGW
    k0 = q0 + NH * P
    vv0 = k0 + NKV * P
    g0 = vv0 + NKV * P
    for b in range(SGW // BLK):
        for c in range(4):
            add(rows(w_in, 4 * c, 4, v0 + b * BLK, BLK))
    for c in range(2):
        add(rows(w_in, 8 * c, 8, vv0, NKV * P))
    for g in range(NKV):
        add(rows(w_in, 0, KD, k0 + g * P, P))
    for h in range(NH):
        add(rows(w_in, 0, KD, q0 + h * P, P))
        add(rows(w_in, 0, KD, u0 + h * P, P))
    for n0 in range(0, KD, 2):
        for n in (n0, n0 + 1):
            add(rows(w_in, 0, KD, g0 + n * P, P))
            add(rows(w_in, 0, KD, g0 + D + n * P, P))
        for n in (n0, n0 + 1):
            add(rows(w_a, 0, 8, n * P, P), rows(w_b, 0, 8, n * P, P))
    for b in range(NB):
        for c in range(4):
            add(rows(w_out, 4 * c, 4, b * BLK, BLK))
    for h in range(2):
        for i in range(HALF * h, HALF * (h + 1)):
            add(rows(w_up, 0, KD, i * P, P))
            add(rows(w_up, 0, KD, DFF + i * P, P))
        for n in range(2):
            for j in range(DOWN_UNITS):
                add(rows(w_down, HALF * h + 2 * j, 2, n * 1024, 1024))
    return np.stack(units)


def kernel(x, norm_mix_pre, w_in, sg_ln_g, sg_ln_b, sg_w, sg_b, attn_sink, w_branch_a, w_branch_b, w_out,
           norm_mix_post, norm_ffn_pre, w_up, conv_w, conv_b, w_down, norm_ffn_post):
    import numpy as np
    import concourse.bacc as bacc
    from concourse.bass_utils import run_bass_kernel_spmd as run

    a = {k: np.asarray(v) for k, v in dict(
        x=x, npre=norm_mix_pre, w_in=w_in, lg=sg_ln_g, lb=sg_ln_b, sg_w=sg_w, sg_b=sg_b, sink=attn_sink,
        wa=w_branch_a, wb=w_branch_b, wo=w_out, npost=norm_mix_post, nfpre=norm_ffn_pre, w_up=w_up,
        cw=conv_w, cb=conv_b, wd=w_down, nfpost=norm_ffn_post).items()}
    ident, mask, rope = _constants()
    taps = np.concatenate([a["cw"][0], a["cb"]], axis=0)
    conv = taps.reshape(4, 2, KF, P).transpose(3, 2, 1, 0)
    arrays = {
        "x": a["x"].reshape(NT, P, D),
        "weights": _pack(a["w_in"][0], a["wa"][0], a["wb"][0], a["wo"][0], a["w_up"][0], a["wd"][0]),
        "gains": np.concatenate([a["npre"], a["npost"], a["nfpre"], a["nfpost"]], axis=0),
        "sg_gb": np.concatenate([a["lg"], a["lb"]], axis=0),
        "sg_wT": a["sg_w"][0].transpose(2, 0, 1),
        "sg_b": a["sg_b"].reshape(1, NG, P),
        "sink": a["sink"].reshape(1, NH),
        "conv": conv,
        "ident": ident, "mask": mask, "rope": rope,
    }
    arrays = {k: np.ascontiguousarray(v) for k, v in arrays.items()}
    nc = bacc.Bacc("TRN2", target_bir_lowering=False, num_devices=1, dynamic_dma_scratch_size=1024)
    args = [nc.dram_tensor(k, v.shape, mybir.dt.from_np(v.dtype), kind="ExternalInput").ap() for k, v in arrays.items()]
    out = nc.dram_tensor("out", (NT, P, D), mybir.dt.float32, kind="ExternalOutput").ap()
    build(nc, *args, out)
    r = run(nc, [arrays], core_ids=[0])
    return r.results[0]["out"].reshape(1, SEQ, D)
```

```python
import concourse.bass as bass
from concourse import mybir

P = 128
D = 2048
SEQ = 256
NT = SEQ // P
KD = D // P
SGW = 1024
NG = SGW // P
NH = 8
NKV = 2
QPK = NH // NKV
DFF = 5632
KF = DFF // P
HALF = KF // 2
ROT = 32
ROPE_THETA = 500000.0
EPS = 1e-6
MASK_VALUE = -1e30
SCALE = float(P) ** -0.5
UNIT = 2048
RING = 4
BLK = 512
NB = D // BLK

T_V, T_KV, T_QU, T_MG, T_OUT, T_FFN = 0, 2, 3, 7, 19, 23
UP_TURNS = KF * 2 // 2 // RING
DOWN_UNITS = HALF // 2
DOWN_TURNS = -(-DOWN_UNITS // RING)
HALF_TURNS = UP_TURNS + 2 * DOWN_TURNS
T_END = T_FFN + 2 * HALF_TURNS
N_UNITS = 224
DOWN_STARTS = [T_FFN + UP_TURNS + h * HALF_TURNS + n * DOWN_TURNS for h in range(2) for n in range(2)]
SHORT_TURNS = [t + DOWN_TURNS - 1 for t in DOWN_STARTS]


def skipped(turn):
    return sum(t < turn for t in SHORT_TURNS)


def exists(turn, slot):
    return turn < T_END and not (slot == RING - 1 and turn in SHORT_TURNS)


def counts_for(turn, slot):
    return 1 if exists(turn, slot + 1) or slot == RING - 1 else 2


def build(nc, x, weights, gains, sg_gb, sg_wT, sg_b, sink, conv, ident_in, mask_in, rope_in, out):
    F32, F32R = mybir.dt.float32, mybir.dt.float32r
    ALU, ACT, AX = mybir.AluOpType, mybir.ActivationFunctionType, mybir.AxisListType

    KB = 1024
    base = 1152
    at = {}

    def region(name, size):
        at[name] = region.top
        region.top += size
    region.top = base
    region("w_hi", RING * 8 * KB)
    region("w_lo", RING * 8 * KB)
    region("raw", RING * 8 * KB)
    region("hT", 32 * KB)
    region("A", 32 * KB)
    region("B", 44 * KB)
    region("gain", 8 * KB)
    region("tmp", 8 * KB)
    region("misc", 2 * KB + 256)

    def sb(name, where, off, shape, dt=F32):
        return nc.alloc_sbuf_tensor_at(name, shape, dt, offset=at[where] + off)

    w_hi = [sb(f"w_hi{s}", "w_hi", s * 8 * KB, [P, UNIT], F32R) for s in range(RING)]
    w_lo = [sb(f"w_lo{s}", "w_lo", s * 8 * KB, [P, UNIT], F32R) for s in range(RING)]
    raw = [sb(f"raw{s}", "raw", s * 8 * KB, [P, UNIT]) for s in range(RING)]
    hT_hi = sb("hT_hi", "hT", 0, [P, KD, SEQ], F32R)
    hT_lo = sb("hT_lo", "hT", 16 * KB, [P, KD, SEQ], F32R)
    xn = sb("xn", "A", 0, [P, NT, D])
    x_tok = sb("x_tok", "A", 16 * KB, [P, NT, D])
    aT_hi = sb("aT_hi", "A", 0, [P, NG, SEQ], F32R)
    aT_lo = sb("aT_lo", "A", 8 * KB, [P, NG, SEQ], F32R)
    bT_hi = sb("bT_hi", "A", 16 * KB, [P, NH, SEQ], F32R)
    bT_lo = sb("bT_lo", "A", 24 * KB, [P, NH, SEQ], F32R)
    o_tok = sb("o_tok", "A", 0, [P, NT, D])
    f_tok = sb("f_tok", "A", 0, [P, NT, D])
    vg = sb("vg", "B", 0, [P, NT, SGW])
    uT = sb("uT", "B", 8 * KB, [P, NG, SEQ])
    vzT = sb("vzT", "B", 16 * KB, [P, NG, SEQ])
    ln_g = sb("ln_g", "B", 24 * KB, [P, SGW])
    ln_b = sb("ln_b", "B", 28 * KB, [P, SGW])
    sgb = sb("sgb", "B", 32 * KB, [P, NG, P])
    sgw = sb("sgw", "B", 36 * KB, [P, NG, P])
    v_tok = sb("v_tok", "B", 40 * KB, [P, NT, NKV * P])
    kT = sb("kT", "B", 42 * KB, [P, NKV, SEQ])
    mT_hi = sb("mT_hi", "B", 0, [P, KD, SEQ], F32R)
    mT_lo = sb("mT_lo", "B", 16 * KB, [P, KD, SEQ], F32R)
    g_ffn = sb("g_ffn", "B", 32 * KB, [P, D])
    act_hi = sb("act_hi", "B", 0, [P, HALF, SEQ], F32R)
    act_lo = sb("act_lo", "B", 22 * KB, [P, HALF, SEQ], F32R)
    gain = sb("gain", "gain", 0, [P, D])
    prob = [sb(f"prob{i}", "tmp", i * 2 * KB, [P, NT, SEQ]) for i in range(2)]
    pT = sb("pT", "tmp", 4 * KB, [P, NT, SEQ])
    qT = [sb(f"qT{i}", "tmp", (6 + i) * KB, [P, SEQ]) for i in range(2)]
    sig = [[sb(f"sig{p}{i}", "tmp", (2 * p + i) * KB, [P, SEQ]) for i in range(2)] for p in range(2)]
    squares = sb("squares", "tmp", 0, [P, BLK])
    diag = [sb(f"diag{t}", "tmp", 4 * KB + 512 * t, [P, P]) for t in range(NT)]
    conv_o = [[sb(f"conv_o{p}{i}", "tmp", (2 * p + i) * KB, [P, SEQ]) for i in range(2)] for p in range(2)]
    gelu_o = [sb(f"gelu_o{p}", "tmp", (4 + p) * KB, [P, SEQ]) for p in range(2)]
    prod = [sb(f"prod{p}", "tmp", (6 + p) * KB, [P, SEQ]) for p in range(2)]
    ident = sb("ident", "misc", 0, [P, P])
    convw = sb("convw", "misc", 512, [P, KF, 2, 4])
    small = sb("small", "misc", 512 + 1408, [P, 64])
    mask = sb("mask", "gain", 0, [P, NT, SEQ])
    ropes = sb("ropes", "gain", 2 * KB, [ROT, 2, SEQ])
    rot = sb("rot", "gain", 4 * KB, [ROT, SEQ])

    ssq, msq, rstd = small[:, 0:2], small[:, 2:4], small[:, 4:6]
    ssq4 = small[:, 6:14]
    neg_half = small[:, 14:15]
    mean_var = [small[:, 16 + 2 * t:18 + 2 * t] for t in range(NT)]
    stats = [small[:, 20 + 12 * t:32 + 12 * t] for t in range(NT)]
    gain_row = sb("gain_row", "tmp", 0, [1, D])
    ones_row = sb("ones_row", "gain", 5 * KB, [1, P])
    smax, negm, psum_p, esink = (small[:, 44 + 2 * i:46 + 2 * i] for i in range(4))
    den, rden = small[:, 52:54], small[:, 54:56]
    sinks = small[:, 56:64]

    def one(tensor, n):
        return tensor[:, bass.ds(n, 1), :].rearrange("p o s -> p (o s)")

    bank = [nc.alloc_psum_tensor(f"bank{i}", [P, BLK], F32) for i in range(8)]

    def sem(name):
        return nc.alloc_semaphore(name)

    raw_ready = [sem(f"raw_ready{s}") for s in range(RING)]
    wh_ready, wl_ready, w_used = sem("wh_ready"), sem("wl_ready"), sem("w_used")
    x_in = [[sem(f"x_in{t}{c}") for c in range(2)] for t in range(NT)]
    gain_rows, pool_lo = sem("gain_rows"), sem("pool_lo")
    ones_set, gain_in, misc_in, tables_in, sg_in = sem("ones_set"), sem("gain_in"), sem("misc_in"), sem("tables_in"), sem("sg_in")
    post_in, ffn_gain_in, x_again, last_gain_in = sem("post_in"), sem("ffn_gain_in"), sem("x_again"), sem("last_gain_in")
    half_set = sem("half_set")
    sq_done, red_done, ms_done, rstd_done = (sem(n) for n in ("sq_done", "red_done", "ms_done", "rstd_done"))
    xn_done, tr_done, hh_done, hl_done = sem("xn_done"), sem("tr_done"), sem("hh_done"), sem("hl_done")
    vg_done, st_done, mv_done = sem("vg_done"), sem("st_done"), sem("mv_done")
    vhat_done, vmul_done, vn_done = sem("vhat_done"), sem("vmul_done"), sem("vn_done")
    vt_done = sem("vt_done")
    rope_copied, rope_turned, rope_sin, rope_cos, rope_done = (
        sem(n) for n in ("rope_copied", "rope_turned", "rope_sin", "rope_cos", "rope_done"))
    u_copied, vz_ready, vz_done = sem("u_copied"), sem("vz_ready"), sem("vz_done")
    sc_ready, sc_read, mx_done, nm_done, exp_done = (
        sem(n) for n in ("sc_ready", "sc_read", "mx_done", "nm_done", "exp_done"))
    den_done, rden_done, p_ready = sem("den_done"), sem("rden_done"), sem("p_ready")
    pt_ready, pt_free, pv_ready, bh_done, bl_free = (
        sem(n) for n in ("pt_ready", "pt_free", "pv_ready", "bh_done", "bl_free"))
    ug_done, a_done, ah_done, al_done = sem("ug_done"), sem("a_done"), sem("ah_done"), sem("al_done")
    sig_done, gated, m_done, mh_done, ml_done = (
        sem(n) for n in ("sig_done", "gated", "m_done", "mh_done", "ml_done"))
    o_ready, o_copied, o_sq = sem("o_ready"), sem("o_copied"), sem("o_sq")
    x1_done, x1_sq, xg_pool, xg_dve, diag_done = (
        sem(n) for n in ("x1_done", "x1_sq", "xg_pool", "xg_dve", "diag_done"))
    c_mid, c_left, c_done, ge_done, pr_done, acth_done, act_done = (
        sem(n) for n in ("c_mid", "c_left", "c_done", "ge_done", "pr_done", "acth_done", "act_done"))
    f_ready, f_done, f_sq, fg_pool, fg_dve, y_done = (
        sem(n) for n in ("f_ready", "f_done", "f_sq", "fg_pool", "fg_dve", "y_done"))
    stored = sem("stored")

    N_PRE, N_V, N_POST, N_FFN, N_LAST = [0, 1], [2, 3], [4, 6], [5, 7], [8, 9]
    V_Q = RING * T_QU
    START_FREE = RING

    def down_bank(h, n):
        return 4 * (1 - h) if n == 0 else 4 * h

    def load_unit(sp, T0, j, r=0):
        turn, slot = T0 + j // RING, j % RING
        if not exists(turn, slot):
            return
        if turn > 0:
            sp.wait_ge(wl_ready, (turn + r) * RING + slot - RING + 1)
        sp.dma_start(raw[slot][:, :], weights[(turn + r) * RING + slot - skipped(turn)]).then_inc(raw_ready[slot], 16)

    def round_unit(act, T0, j, r=0):
        turn, slot = T0 + j // RING, j % RING
        if not exists(turn, slot):
            return
        v = (turn + r) * RING + slot
        act.wait_ge(raw_ready[slot], (turn + r + 1 - (skipped(turn) if slot == RING - 1 else 0)) * 16)
        if turn > 0:
            act.wait_ge(w_used, v - RING + 1)
        act.activation(w_hi[slot][:, :], raw[slot][:, :], ACT.Copy).then_inc(wh_ready, counts_for(turn, slot))

    def rest_unit(dve, T0, j, r=0):
        turn, slot = T0 + j // RING, j % RING
        if not exists(turn, slot):
            return
        dve.wait_ge(wh_ready, (turn + r) * RING + slot + 1)
        count = 2 if (turn, slot) == (0, 3) else counts_for(turn, slot)
        dve.tensor_tensor(w_lo[slot][:, :], raw[slot][:, :], w_hi[slot][:, :], ALU.subtract).then_inc(wl_ready, count)

    block = nc.Block()
    with block:
        @block.sync
        def _(sp):
            half = D // 2
            sp.dma_start(gain_row[:, :], gains[0:1, :]).then_inc(gain_in, 16)
            for c in range(2):
                sp.dma_start(x_tok[:, 0, c * half:(c + 1) * half], x[0][:, c * half:(c + 1) * half]).then_inc(x_in[0][c], 16)
            load_unit(sp, 0, 0)
            load_unit(sp, 0, 1)
            for c in range(2):
                sp.dma_start(x_tok[:, 1, c * half:(c + 1) * half], x[1][:, c * half:(c + 1) * half]).then_inc(x_in[1][c], 16)
            load_unit(sp, 0, 2)
            load_unit(sp, 0, 3)
            sp.dma_start(ln_g[:, :], sg_gb[0:1, :].partition_broadcast(P)).then_inc(sg_in, 16)
            sp.dma_start(ln_b[:, :], sg_gb[1:2, :].partition_broadcast(P)).then_inc(sg_in, 16)
            sp.dma_start(sgb[:, :, :], sg_b.partition_broadcast(P)).then_inc(sg_in, 16)
            sp.dma_start(sgw[:, :, :], sg_wT).then_inc(sg_in, 16)
            sp.dma_start(sinks, sink.partition_broadcast(P)).then_inc(sg_in, 16)
            sp.dma_start(convw[:, :, :, :], conv).then_inc(sg_in, 16)
            for j in range(RING):
                if j == 2:
                    sp.wait_ge(pool_lo, 1)
                load_unit(sp, 1, j)
            sp.dma_start(mask[:, :, :], mask_in).then_inc(tables_in, 16)
            sp.dma_start(ropes[:, :, :], rope_in).then_inc(tables_in, 16)
            with sp.Fori(0, T_MG + 4 - 2) as i:
                for j in range(RING):
                    load_unit(sp, 2, j, i)
            sp.wait_ge(sc_read, NH)
            sp.wait_ge(rope_done, NKV + NH)
            sp.dma_start(gain[:, :], gains[1:2, :].partition_broadcast(P)).then_inc(post_in, 16)
            with sp.Fori(0, T_OUT + 2 - (T_MG + 4)) as i:
                for j in range(RING):
                    load_unit(sp, T_MG + 4, j, i)
            sp.wait_ge(w_used, RING * T_OUT)
            for t in range(NT):
                sp.dma_start(x_tok[:, t, :], x[t]).then_inc(x_again, 16)
            sp.dma_start(g_ffn[:, :], gains[2:3, :].partition_broadcast(P)).then_inc(ffn_gain_in, 16)
            with sp.Fori(0, T_FFN - (T_OUT + 2)) as i:
                for j in range(RING):
                    load_unit(sp, T_OUT + 2, j, i)
            for h in range(2):
                T0 = T_FFN + h * HALF_TURNS
                with sp.Fori(0, UP_TURNS) as i:
                    for j in range(RING):
                        load_unit(sp, T0, j, i)
                if h == 0:
                    sp.wait_ge(o_copied, NB * NT)
                    sp.dma_start(gain[:, :], gains[3:4, :].partition_broadcast(P)).then_inc(last_gain_in, 16)
                for n in range(2):
                    for j in range(DOWN_TURNS * RING):
                        load_unit(sp, T0 + UP_TURNS + n * DOWN_TURNS, j)
            for t in range(NT):
                for c in range(2):
                    col = slice(2 * c * BLK, 2 * (c + 1) * BLK)
                    sp.wait_ge(y_done, NB * t + 2 * c + 2)
                    sp.dma_start(out[t][:, col], f_tok[:, t, col]).then_inc(stored, 16)
            sp.wait_ge(stored, 16 * NT * 2)

        @block.gpsimd
        def _(pool):
            pool.memset(ones_row[:, :], 1.0).then_inc(ones_set, 1)
            pool.memset(neg_half, -0.5).then_inc(half_set, 1)
            pool.wait_ge(half_set, 1)

            def power(n, t):
                pool.wait_ge(ms_done, n[t] + 1)
                pool.tensor_tensor(rstd[:, t:t + 1], msq[:, t:t + 1], neg_half, ALU.pow).then_inc(rstd_done, 1)

            def rope(n, dst, ahead=0):
                c = n + 1 + ahead
                pool.wait_ge(rope_turned, c)
                pool.tensor_tensor(rot[:, :], rot[:, :], ropes[:, 1, :], ALU.mult).then_inc(rope_sin, 1)
                pool.tensor_tensor(dst, dst, ropes[:, 0, :], ALU.mult).then_inc(rope_cos, 1)
                pool.wait_ge(rope_sin, c)
                pool.wait_ge(rope_cos, c)
                pool.tensor_tensor(dst, dst, rot[:, :], ALU.add).then_inc(rope_done, 1)

            power(N_PRE, 0)
            power(N_PRE, 1)
            pool.wait_ge(wh_ready, 3)
            pool.tensor_tensor(w_lo[2][:, :], raw[2][:, :], w_hi[2][:, :], ALU.subtract).then_inc(pool_lo, 1)
            pool.wait_ge(sg_in, 16 * 6)
            for t in range(NT):
                power(N_V, t)
                pool.wait_ge(vhat_done, t + 1)
                pool.tensor_tensor(vg[:, t, :], vg[:, t, :], ln_g[:, :], ALU.mult).then_inc(vmul_done, 1)
                pool.wait_ge(vmul_done, t + 1)
                pool.tensor_tensor(vg[:, t, :], vg[:, t, :], ln_b[:, :], ALU.add).then_inc(vn_done, 1)
            pool.wait_ge(tables_in, 32)
            for g in range(NKV):
                rope(g, kT[0:ROT, g, :])
            with pool.Fori(0, NH // 2) as i:
                for p in range(2):
                    rope(NKV + p, qT[p][0:ROT, :], 2 * i)
            pool.wait_ge(ffn_gain_in, 16)
            for t in range(NT):
                power(N_POST, t)
                for b in range(2):
                    col = slice(b * BLK, (b + 1) * BLK)
                    pool.wait_ge(x1_done, NB * t + b + 1)
                    pool.tensor_tensor(o_tok[:, t, col], x_tok[:, t, col], g_ffn[:, col], ALU.mult).then_inc(xg_pool, 1)
                power(N_FFN, t)
            pool.wait_ge(last_gain_in, 16)
            for t in range(NT):
                for b in range(2):
                    col = slice(b * BLK, (b + 1) * BLK)
                    pool.wait_ge(f_sq, 2 * t + b + 1)
                    pool.tensor_tensor(f_tok[:, t, col], f_tok[:, t, col], gain[:, col], ALU.mult).then_inc(fg_pool, 1)
            for t in range(NT):
                power(N_LAST, t)

        @block.scalar
        def _(act):
            def square(t, b, src, junk, size, done):
                act.activation(junk, src[:, t, b * size:(b + 1) * size], ACT.Square,
                               accum_out=ssq4[:, NB * t + b:NB * t + b + 1]).then_inc(done, 1)

            def turn_hi(first_bank, n, t, blocks=range(NB)):
                for b in blocks:
                    act.wait_ge(tr_done, n + NB * t + b + 1)
                    act.activation(hT_hi[:, 4 * b:4 * b + 4, t * P:(t + 1) * P],
                                   bank[first_bank + b][:, :].rearrange("p (k s) -> p k s", k=4),
                                   ACT.Copy).then_inc(hh_done, 1)

            def rope_copy(v, b, dst, n):
                act.wait_ge(w_used, v + 1)
                act.activation(dst, bank[b][:, 0:SEQ], ACT.Copy).then_inc(rope_copied, 1)

            def exps(h, p):
                act.wait_ge(nm_done, h + 1)
                for t in range(NT):
                    act.activation(prob[p][:, t, :], prob[p][:, t, :], ACT.Exp, bias=negm[:, t:t + 1],
                                   accum_out=psum_p[:, t:t + 1]).then_inc(exp_done, 1)
                act.activation(esink, negm, ACT.Exp, bias=sinks[:, bass.ds(h, 1)]).then_inc(exp_done, 1)

            def b_hi(h):
                act.wait_ge(pv_ready, h + 1)
                act.activation(one(bT_hi, h), bank[6][:, 0:SEQ], ACT.Copy).then_inc(bh_done, 1)

            def head(h, p, T0, r, first=False, second=False):
                q = V_Q + 2 * h
                round_unit(act, T0, 2 * p + 3, r)
                if not (first or second):
                    act.wait_ge(sc_ready, h - 1)
                rope_copy(q, p, qT[p][:, :], h)
                if not first:
                    exps(h - 1, 1 - p)
                round_unit(act, T0, 2 * p + 4, r)
                act.wait_ge(w_used, q + 2)
                act.activation(one(uT, h), bank[2 + p][:, 0:SEQ], ACT.Copy).then_inc(u_copied, 1)
                if not (first or second):
                    b_hi(h - 2)

            act.dma_start(ident[:, :], ident_in).then_inc(misc_in, 16)
            for t in range(NT):
                for c in range(2):
                    act.wait_ge(x_in[t][c], 16)
                    square(t, c, x_tok, xn[:, t, c * D // 2:(c + 1) * D // 2], D // 2, sq_done)
                if t == 0:
                    round_unit(act, 0, 0)
                    turn_hi(0, 0, 0, [0, 1])
                    round_unit(act, 0, 1)
            turn_hi(0, 0, 0, [2, 3])
            round_unit(act, 0, 2)
            turn_hi(4, 0, 1)
            round_unit(act, 0, 3)
            for b in range(2):
                for j in range(RING):
                    if b + j > 0:
                        round_unit(act, b, j + 3)
                act.wait_ge(w_used, RING * (b + 1))
                for t in range(NT):
                    act.activation(vg[:, t, b * BLK:(b + 1) * BLK], bank[2 * b + t][:, :], ACT.Gelu_apprx_tanh).then_inc(vg_done, 1)
            round_unit(act, T_KV, 3)
            round_unit(act, T_KV, 4)
            act.wait_ge(w_used, RING * T_KV + 2)
            for t in range(NT):
                act.activation(v_tok[:, t, :], bank[4 + t][:, 0:SEQ], ACT.Copy).then_inc(vt_done, 1)
            for g in range(NKV):
                round_unit(act, T_KV, 5 + g)
                rope_copy(RING * T_KV + 2 + g, 6 + g, kT[:, g, :], g)
            act.wait_ge(sg_in, 16 * 6)
            head(0, 0, T_QU, 0, first=True)
            head(1, 1, T_QU, 0, second=True)
            with act.Fori(1, NH // 2) as i:
                for p in range(2):
                    head(2 * i + p, p, T_QU, i)

            def sigmoid(n, i, p, v, guard=True):
                act.wait_ge(w_used, v + 1)
                if guard:
                    act.wait_ge(ml_done, n - 1)
                act.activation(sig[p][i][:, :], bank[2 * p + i][:, 0:SEQ], ACT.Sigmoid).then_inc(sig_done, 1)

            def m_hi(n, p):
                act.wait_ge(m_done, n + 1)
                act.activation(one(mT_hi, n), sig[p][0][:, :], ACT.Copy).then_inc(mh_done, 1)

            def pair(T0, j0, r, n, first=False):
                v = (T0 + r) * RING + j0
                if first:
                    round_unit(act, T0, j0 + 3, r)
                    exps(NH - 1, 1)
                    round_unit(act, T0, j0 + 4, r)
                    act.wait_ge(u_copied, NG)
                    act.activation(uT[:, :, :], uT[:, :, :], ACT.Gelu_apprx_tanh).then_inc(ug_done, 1)
                    b_hi(NH - 2)
                    round_unit(act, T0, j0 + 5, r)
                    act.wait_ge(a_done, 1)
                    act.activation(aT_hi[:, :, :], uT[:, :, :], ACT.Copy).then_inc(ah_done, 1)
                    b_hi(NH - 1)
                    act.wait_ge(pt_ready, NH)
                    for g in range(4):
                        if g == 3:
                            round_unit(act, T0, j0 + 6, r)
                        sigmoid(n + g // 2, g % 2, g // 2, v + g, guard=False)
                else:
                    for g in range(4):
                        round_unit(act, T0, j0 + 3 + g, r)
                        sigmoid(n + g // 2, g % 2, g // 2, v + g)
                for p in range(2):
                    round_unit(act, T0, j0 + 7 + p, r)
                    m_hi(n + p, p)

            pair(T_MG, 0, 0, 0, first=True)
            pair(T_MG, 6, 0, 2)
            with act.Fori(1, KD // 4) as i:
                pair(T_MG, 0, 3 * i, 4 * i)
                pair(T_MG, 6, 3 * i, 4 * i + 2)

            for b in range(NB):
                round_unit(act, T_OUT + b, 3)
                for t in range(NT):
                    if t == 0:
                        act.wait_ge(o_ready, b + 1)
                    else:
                        round_unit(act, T_OUT + b, 4)
                        round_unit(act, T_OUT + b, 5)
                        act.wait_ge(w_used, RING * (T_OUT + b + 1))
                    if b + t > 0:
                        act.wait_ge(o_sq, 2 * b + t)
                    if (b, t) == (NB - 1, 1):
                        act.wait_ge(x1_sq, NB)
                    act.activation(squares[:, :], bank[2 * (b % 2) + t][:, :], ACT.Square,
                                   accum_out=ssq4[:, NB * t + b:NB * t + b + 1]).then_inc(o_sq, 1)
                    if b == NB - 1:
                        if t == 1:
                            turn_hi(4, NB * NT, 0, [0, 1])
                        act.wait_ge(o_sq, 2 * b + t + 1)
                        for c in range(NB):
                            act.wait_ge(x1_done, NB * t + c + 1)
                            if c > 0:
                                act.wait_ge(x1_sq, NB * t + c)
                            square(t, c, x_tok, squares[:, :], BLK, x1_sq)
                if b < NB - 1:
                    round_unit(act, T_OUT + b, 6)
            turn_hi(4, NB * NT, 0, [2, 3])
            round_unit(act, T_OUT + NB - 1, 6)
            turn_hi(0, NB * NT, 1)

            act.wait_ge(x1_sq, NB * NT)

            def up(T0, j0, r, pp, h):
                p = (j0 // 2) % 2
                v = (T0 + r) * RING + j0
                for i in range(2):
                    round_unit(act, T0, j0 + i + 3, r)
                    act.wait_ge(w_used, v + i + 1)
                    act.wait_ge(pr_done, pp + 1)
                    act.activation(conv_o[p][i][:, :], bank[4 * h + 2 * p + i][:, 0:SEQ], ACT.Identity,
                                   scale=convw[:, bass.ds(pp, 1), i, 1], bias=convw[:, bass.ds(pp, 1), i, 3]).then_inc(c_mid, 1)
                act.wait_ge(c_done, START_FREE + 2 * pp + 1)
                act.activation(gelu_o[p][:, :], conv_o[p][0][:, :], ACT.Gelu_apprx_tanh).then_inc(ge_done, 1)
                act.wait_ge(pr_done, pp + 1 + 2)
                act.activation(one(act_hi, pp - HALF * h), prod[p][:, :], ACT.Copy).then_inc(acth_done, 1)

            for h in range(2):
                T0 = T_FFN + h * HALF_TURNS
                with act.Fori(0, UP_TURNS) as i:
                    for q in range(2):
                        up(T0, 2 * q, i, 2 * i + q + HALF * h, h)
                for n in range(2):
                    for j in range(DOWN_TURNS * RING):
                        round_unit(act, T0 + UP_TURNS + n * DOWN_TURNS, j + 3)
            for n in range(2):
                for t in range(NT):
                    for c in range(2):
                        b = 2 * n + c
                        act.wait_ge(f_done, 8 + 4 * n + 2 * t + c + 1)
                        if n + t + c > 0:
                            act.wait_ge(f_sq, 4 * n + 2 * t + c)
                        act.activation(squares[:, :], f_tok[:, t, b * BLK:(b + 1) * BLK], ACT.Square,
                                       accum_out=ssq4[:, NB * t + b:NB * t + b + 1]).then_inc(f_sq, 1)

        @block.vector
        def _(dve):
            def mean_square(t):
                dve.tensor_scalar(msq[:, t:t + 1], ssq[:, t:t + 1], 1.0 / D, EPS, ALU.mult, ALU.add).then_inc(ms_done, 1)

            def mean_square_of(t, parts, count):
                dve.tensor_reduce(ssq[:, t:t + 1], ssq4[:, NB * t:NB * t + parts], AX.X, ALU.add).then_inc(red_done, 1)
                dve.wait_ge(red_done, count)
                mean_square(t)

            def turn_lo(first_bank, n, t, blocks=range(NB)):
                for b in blocks:
                    dst = (slice(None), slice(4 * b, 4 * b + 4), slice(t * P, (t + 1) * P))
                    dve.wait_ge(hh_done, n + NB * t + b + 1)
                    dve.tensor_tensor(hT_lo[dst], bank[first_bank + b][:, :].rearrange("p (k s) -> p k s", k=4),
                                      hT_hi[dst], ALU.subtract).then_inc(hl_done, 1)

            def turned(n, src):
                dve.wait_ge(rope_copied, n + 1)
                if not isinstance(n, int) or n > 0:
                    dve.wait_ge(rope_done, n)
                dve.stream_shuffle(rot[:, :], src, [(i + ROT // 2) % ROT for i in range(ROT)]).then_inc(rope_turned, 1)

            def scores(h, p, guard=True):
                dve.wait_ge(sc_ready, h + 1)
                if guard:
                    dve.wait_ge(pt_ready, h - 1)
                dve.scalar_tensor_tensor(prob[p][:, :, :], bank[4][:, :].rearrange("p (t s) -> p t s", t=NT), SCALE,
                                         mask[:, :, :], ALU.mult, ALU.add).then_inc(sc_read, 1)
                dve.wait_ge(sc_read, h + 1)
                dve.tensor_reduce(smax, prob[p][:, :, :], AX.X, ALU.max).then_inc(mx_done, 1)
                dve.wait_ge(mx_done, h + 1)
                dve.tensor_scalar(negm, smax, sinks[:, bass.ds(h, 1)], -1.0, ALU.max, ALU.mult).then_inc(nm_done, 1)

            def probabilities(h, p):
                dve.wait_ge(exp_done, 3 * h + 3)
                dve.tensor_tensor(den, psum_p, esink, ALU.add).then_inc(den_done, 1)
                dve.wait_ge(den_done, h + 1)
                dve.reciprocal(rden, den).then_inc(rden_done, 1)
                dve.wait_ge(rden_done, h + 1)
                for t in range(NT):
                    dve.tensor_scalar(prob[p][:, t, :], prob[p][:, t, :], rden[:, t:t + 1], None, ALU.mult).then_inc(p_ready, 1)

            def copy_pT(h, guard=True):
                dve.wait_ge(pt_ready, h + 1)
                if guard:
                    dve.wait_ge(pv_ready, h)
                dve.tensor_copy(pT[:, :, :], bank[5][:, :].rearrange("p (k s) -> p k s", k=NT)).then_inc(pt_free, 1)

            def vz(h):
                dve.wait_ge(vz_ready, h + 1)
                dve.tensor_tensor(vzT[:, bass.ds(h, 1), :].rearrange("p g (c t) -> p (g c) t", c=NT),
                                  bank[7][:, 0:SEQ].rearrange("p (c t) -> p c t", c=NT),
                                  sgb[:, bass.ds(h, 1), :].broadcast_to([P, NT, P]), ALU.add).then_inc(vz_done, 1)

            def b_lo(h):
                dve.wait_ge(bh_done, h + 1)
                dve.tensor_tensor(one(bT_lo, h), bank[6][:, 0:SEQ], one(bT_hi, h), ALU.subtract).then_inc(bl_free, 1)

            def head(h, p, T0, r, first=False, second=False, third=False):
                rest_unit(dve, T0, 2 * p + 3, r)
                turned(NKV + h, qT[p][0:ROT, :])
                if not first:
                    scores(h - 1, 1 - p, guard=not (second or third))
                if not (first or second):
                    copy_pT(h - 2, guard=not third)
                rest_unit(dve, T0, 2 * p + 4, r)
                if not first:
                    probabilities(h - 1, 1 - p)
                vz(h)
                if not (first or second):
                    b_lo(h - 2)

            def mixer_norm(t):
                dve.wait_ge(sq_done, 2 * t + 2)
                mean_square_of(t, 2, t + 1)

            def mixer_scale(t, b):
                col = slice(b * BLK, (b + 1) * BLK)
                dve.scalar_tensor_tensor(xn[:, t, col], x_tok[:, t, col], rstd[:, t:t + 1], bank[4 + b][:, :],
                                         ALU.mult, ALU.mult).then_inc(xn_done, 1)

            mixer_norm(0)
            dve.wait_ge(rstd_done, 1)
            for b in range(NB):
                dve.wait_ge(gain_rows, b + 1)
                mixer_scale(0, b)
            rest_unit(dve, 0, 0)
            turn_lo(0, 0, 0, [0, 1])
            rest_unit(dve, 0, 1)
            mixer_norm(1)
            dve.wait_ge(rstd_done, 2)
            for b in range(NB):
                mixer_scale(1, b)
            turn_lo(0, 0, 0, [2, 3])
            turn_lo(4, 0, 1)
            rest_unit(dve, 0, 3)
            for b in range(2):
                for j in range(RING):
                    if b + j > 0:
                        rest_unit(dve, b, j + 3)
                for t in range(NT):
                    dve.wait_ge(vg_done, NT * b + t + 1)
                    dve.bn_stats(stats[t][:, 6 * b:6 * b + 6], vg[:, t, b * BLK:(b + 1) * BLK]).then_inc(st_done, 1)
            rest_unit(dve, T_KV, 3)
            for t in range(NT):
                dve.wait_ge(st_done, 3 + t)
                dve.bn_aggr(mean_var[t], stats[t]).then_inc(mv_done, 1)
                dve.wait_ge(mv_done, t + 1)
                dve.tensor_scalar(msq[:, t:t + 1], mean_var[t][:, 1:2], EPS, None, ALU.add).then_inc(ms_done, 1)
            for t in range(NT):
                dve.wait_ge(rstd_done, N_V[t] + 1)
                dve.tensor_scalar(vg[:, t, :], vg[:, t, :], mean_var[t][:, 0:1], rstd[:, t:t + 1],
                                  ALU.subtract, ALU.mult).then_inc(vhat_done, 1)
            rest_unit(dve, T_KV, 4)
            for g in range(NKV):
                rest_unit(dve, T_KV, 5 + g)
                turned(g, kT[0:ROT, g, :])
            dve.wait_ge(tables_in, 32)
            dve.wait_ge(sg_in, 16 * 6)
            dve.sem_inc(pt_free, 1)
            dve.sem_inc(bl_free, 1)
            for h in range(NH):
                head(h, h % 2, T_QU + h // 2, 0, first=h == 0, second=h == 1, third=h == 2)

            def merged(n, p):
                for i in range(2):
                    dve.tensor_tensor(sig[p][i][:, :], sig[p][i][:, :], bank[4 + 2 * p + i][:, 0:SEQ], ALU.mult).then_inc(gated, 1)
                dve.wait_ge(gated, 2 * n + 2)
                dve.tensor_tensor(sig[p][0][:, :], sig[p][0][:, :], sig[p][1][:, :], ALU.add).then_inc(m_done, 1)
                dve.wait_ge(mh_done, n + 1)
                dve.tensor_tensor(one(mT_lo, n), sig[p][0][:, :], one(mT_hi, n), ALU.subtract).then_inc(ml_done, 1)

            def pair(T0, j0, r, n, first=False):
                v = (T0 + r) * RING + j0
                if first:
                    rest_unit(dve, T0, j0 + 3, r)
                    scores(NH - 1, 1)
                    copy_pT(NH - 2)
                    probabilities(NH - 1, 1)
                    rest_unit(dve, T0, j0 + 4, r)
                    b_lo(NH - 2)
                    copy_pT(NH - 1)
                    rest_unit(dve, T0, j0 + 5, r)
                    dve.wait_ge(ug_done, 1)
                    dve.wait_ge(vz_done, NG)
                    dve.tensor_tensor(uT[:, :, :], uT[:, :, :], vzT[:, :, :], ALU.mult).then_inc(a_done, 1)
                    dve.wait_ge(ah_done, 1)
                    dve.tensor_tensor(aT_lo[:, :, :], uT[:, :, :], aT_hi[:, :, :], ALU.subtract).then_inc(al_done, 1)
                    b_lo(NH - 1)
                    rest_unit(dve, T0, j0 + 6, r)
                else:
                    for g in range(4):
                        rest_unit(dve, T0, j0 + 3 + g, r)
                for p in range(2):
                    rest_unit(dve, T0, j0 + 7 + p, r)
                    dve.wait_ge(sig_done, 2 * (n + p) + 2)
                    dve.wait_ge(w_used, v + 4 + p + 1)
                    merged(n + p, p)

            pair(T_MG, 0, 0, 0, first=True)
            pair(T_MG, 6, 0, 2)
            with dve.Fori(1, KD // 4) as i:
                pair(T_MG, 0, 3 * i, 4 * i)
                pair(T_MG, 6, 3 * i, 4 * i + 2)

            def residual(t):
                if t == 1:
                    turn_lo(4, NB * NT, 0, [0])
                dve.wait_ge(x_again, 16 * NT)
                dve.wait_ge(rstd_done, N_POST[t] + 1)
                dve.wait_ge(o_copied, 2 * (NB - 1) + t + 1)
                for b in range(NB):
                    col = slice(b * BLK, (b + 1) * BLK)
                    dve.scalar_tensor_tensor(x_tok[:, t, col], o_tok[:, t, col], rstd[:, t:t + 1], x_tok[:, t, col],
                                             ALU.mult, ALU.add).then_inc(x1_done, 1)
                dve.wait_ge(ffn_gain_in, 16)
                for b in range(2, NB):
                    col = slice(b * BLK, (b + 1) * BLK)
                    dve.wait_ge(x1_done, NB * t + b + 1)
                    dve.tensor_tensor(o_tok[:, t, col], x_tok[:, t, col], g_ffn[:, col], ALU.mult).then_inc(xg_dve, 1)
                if t == 1:
                    turn_lo(4, NB * NT, 0, [1])
                dve.wait_ge(x1_sq, NB * (t + 1))
                mean_square_of(t, NB, NT + 2 * t + 2)
                if t == 1:
                    turn_lo(4, NB * NT, 0, [2])
                dve.wait_ge(rstd_done, N_FFN[t] + 1)
                dve.tensor_scalar(diag[t][:, :], ident[:, :], rstd[:, t:t + 1], None, ALU.mult).then_inc(diag_done, 1)

            dve.wait_ge(post_in, 16)
            for b in range(NB):
                rest_unit(dve, T_OUT + b, 3)
                for t in range(NT):
                    if t == 1:
                        rest_unit(dve, T_OUT + b, 4)
                        rest_unit(dve, T_OUT + b, 5)
                    dve.wait_ge(o_sq, 2 * b + t + 1)
                    if b == NB - 1:
                        mean_square_of(t, NB, NT + 2 * t + 1)
                    dve.tensor_tensor(o_tok[:, t, b * BLK:(b + 1) * BLK], bank[2 * (b % 2) + t][:, :],
                                      gain[:, b * BLK:(b + 1) * BLK], ALU.mult).then_inc(o_copied, 1)
                    if b == NB - 1:
                        residual(t)
                if b < NB - 1:
                    rest_unit(dve, T_OUT + b, 6)
            turn_lo(4, NB * NT, 0, [3])
            turn_lo(0, NB * NT, 1)
            rest_unit(dve, T_OUT + NB - 1, 6)

            dve.sem_inc(c_done, START_FREE)
            dve.sem_inc(pr_done, 2)

            def up(T0, j0, r, pp, h):
                p = (j0 // 2) % 2
                for i in range(2):
                    c = conv_o[p][i]
                    src = bank[4 * h + 2 * p + i]
                    rest_unit(dve, T0, j0 + i + 3, r)
                    dve.wait_ge(c_mid, 2 * pp + i + 1)
                    dve.scalar_tensor_tensor(c[:, 1:SEQ], src[:, 0:SEQ - 1], convw[:, bass.ds(pp, 1), i, 0], c[:, 1:SEQ],
                                             ALU.mult, ALU.add).then_inc(c_left, 1)
                    dve.wait_ge(c_left, 2 * pp + i + 1)
                    dve.scalar_tensor_tensor(c[:, 0:SEQ - 1], src[:, 1:SEQ], convw[:, bass.ds(pp, 1), i, 2], c[:, 0:SEQ - 1],
                                             ALU.mult, ALU.add).then_inc(c_done, 1)
                dve.wait_ge(ge_done, pp + 1)
                dve.wait_ge(c_done, START_FREE + 2 * pp + 2)
                dve.tensor_tensor(prod[p][:, :], gelu_o[p][:, :], conv_o[p][1][:, :], ALU.mult).then_inc(pr_done, 1)
                dve.wait_ge(acth_done, pp + 1)
                dve.tensor_tensor(one(act_lo, pp - HALF * h), prod[p][:, :], one(act_hi, pp - HALF * h),
                                  ALU.subtract).then_inc(act_done, 1)

            def f_block(h, n, tiles=range(NT)):
                for t in tiles:
                    if tiles == [0]:
                        dve.wait_ge(f_ready, 1)
                    else:
                        dve.wait_ge(w_used, RING * (T_FFN + h * HALF_TURNS + UP_TURNS + (n + 1) * DOWN_TURNS))
                    for c in range(2):
                        col = slice((2 * n + c) * BLK, (2 * n + c + 1) * BLK)
                        src = bank[down_bank(h, n) + 2 * t + c]
                        if h == 0:
                            dve.tensor_copy(f_tok[:, t, col], src[:, :]).then_inc(f_done, 1)
                        else:
                            dve.wait_ge(f_done, 4 * n + 2 * t + c + 1)
                            dve.tensor_tensor(f_tok[:, t, col], f_tok[:, t, col], src[:, :], ALU.add).then_inc(f_done, 1)

            for h in range(2):
                T0 = T_FFN + h * HALF_TURNS
                with dve.Fori(0, UP_TURNS) as i:
                    for q in range(2):
                        up(T0, 2 * q, i, 2 * i + q + HALF * h, h)
                for n in range(2):
                    for j in range(DOWN_TURNS * RING):
                        rest_unit(dve, T0 + UP_TURNS + n * DOWN_TURNS, j + 3)
                        if j == 0 and n == 1:
                            f_block(h, 0)
                if h == 0:
                    f_block(h, 1)
            dve.wait_ge(last_gain_in, 16)
            for t in range(NT):
                f_block(1, 1, [t])
                for c in range(2):
                    col = slice((2 + c) * BLK, (3 + c) * BLK)
                    dve.wait_ge(f_sq, 4 + 2 * t + c + 1)
                    dve.tensor_tensor(f_tok[:, t, col], f_tok[:, t, col], gain[:, col], ALU.mult).then_inc(fg_dve, 1)
                    if c == 1:
                        mean_square_of(t, NB, 3 * NT + t + 1)
                dve.wait_ge(rstd_done, N_LAST[t] + 1)
                dve.wait_ge(fg_pool, 2 * t + 2)
                dve.wait_ge(fg_dve, 2 * t + 2)
                for b in range(NB):
                    col = slice(b * BLK, (b + 1) * BLK)
                    dve.scalar_tensor_tensor(f_tok[:, t, col], f_tok[:, t, col], rstd[:, t:t + 1], x_tok[:, t, col],
                                             ALU.mult, ALU.add).then_inc(y_done, 1)

        @block.tensor
        def _(pe):
            def passes(dst, a_hi, a_lo, b_hi, b_lo, first, last):
                pe.matmul(dst, a_hi, b_hi, start=first, stop=False)
                pe.matmul(dst, a_hi, b_lo, start=False, stop=False)
                return pe.matmul(dst, a_lo, b_hi, start=False, stop=last)

            def arrived(T0, j, r=0):
                pe.wait_ge(wl_ready, (T0 + r) * RING + j + 1)

            def stationary(T0, j, r, dst, rhs_hi, rhs_lo, ks=range(KD), done=None, turned=0):
                hi = w_hi[j % RING][:, :].rearrange("p (k m) -> p k m", m=P)
                lo = w_lo[j % RING][:, :].rearrange("p (k m) -> p k m", m=P)
                for k in ks:
                    i = k - ks[0]
                    if turned and k % 4 == 0:
                        pe.wait_ge(hl_done, turned + k // 4 + 1)
                    last = passes(dst, hi[:, k, :], lo[:, k, :], rhs_hi[:, i, :], rhs_lo[:, i, :], i == 0, i == len(ks) - 1)
                if done is None:
                    last.then_inc(w_used, 1)

            def tokens(T0, banks, src_hi, src_lo, waits=None, ready=None, order=None):
                for t, c in order or [(t, c) for t in range(NT) for c in range(RING)]:
                    if t == 0:
                        arrived(T0, c)
                    if waits:
                        waits(t, c)
                    hi = w_hi[c][:, :].rearrange("p (k n) -> p k n", n=BLK)
                    lo = w_lo[c][:, :].rearrange("p (k n) -> p k n", n=BLK)
                    for kk in range(4):
                        k = 4 * c + kk
                        tt = slice(t * P, (t + 1) * P)
                        last = passes(banks[t][:, :], src_hi[:, k, tt], src_lo[:, k, tt], hi[:, kk, :], lo[:, kk, :],
                                      k == 0, k == KD - 1)
                    if t == NT - 1:
                        last.then_inc(w_used, 1)
                    elif ready is not None and c == RING - 1:
                        last.then_inc(ready, 1)

            def turn_block(src, first_bank, t, b, rhs):
                for k in range(4):
                    dst = bank[first_bank + b][:, k * P:(k + 1) * P]
                    part = src[:, t, (4 * b + k) * P:(4 * b + k + 1) * P]
                    if rhs is ident:
                        last = pe.transpose(dst, part, ident[:, :])
                    else:
                        last = pe.matmul(dst, part, rhs[:, :], start=True, stop=True)
                last.then_inc(tr_done, 1)

            def scores(h, p, guard=True):
                pe.wait_ge(rope_done, NKV + h + 1)
                if guard:
                    pe.wait_ge(sc_read, h)
                g = kv_of(h, p)
                for t in range(NT):
                    last = pe.matmul(bank[4][:, t * SEQ:(t + 1) * SEQ], qT[p][:, t * P:(t + 1) * P], g, start=True, stop=True)
                last.then_inc(sc_ready, 1)

            def kv_of(h, p):
                return kT[:, bass.ds(h // QPK, 1), :].rearrange("p g s -> p (g s)")

            def turn_probs(h, p):
                pe.wait_ge(p_ready, 2 * h + 2)
                pe.wait_ge(pt_free, h + 1)
                for t in range(NT):
                    for k in range(NT):
                        last = pe.transpose(bank[5][:, k * SEQ + t * P:k * SEQ + (t + 1) * P],
                                            prob[p][:, t, k * P:(k + 1) * P], ident[:, :])
                last.then_inc(pt_ready, 1)

            def values(h, g):
                pe.wait_ge(pt_free, h + 2)
                pe.wait_ge(bl_free, h + 1)
                for k in range(NT):
                    last = pe.matmul(bank[6][:, 0:SEQ], v_tok[:, k, g * P:(g + 1) * P], pT[:, k, :],
                                     start=k == 0, stop=k == NT - 1)
                last.then_inc(pv_ready, 1)

            def spatial(h, guard=True):
                if guard:
                    pe.wait_ge(vz_done, h)
                for c in range(NT):
                    last = pe.matmul(bank[7][:, c * P:(c + 1) * P], vg[:, c, h * P:(h + 1) * P], sgw[:, h, :],
                                     start=True, stop=True)
                last.then_inc(vz_ready, 1)

            def head(h, T0):
                p = h % 2
                r = h // 2
                arrived(T0, 2 * p, r)
                if h >= 2:
                    pe.wait_ge(rope_copied, NKV + h - 1)
                stationary(T0, 2 * p, r, bank[p][:, 0:SEQ], hT_hi, hT_lo)
                if h >= 1:
                    scores(h - 1, 1 - p, guard=h >= 2)
                if h >= 2:
                    turn_probs(h - 2, p)
                arrived(T0, 2 * p + 1, r)
                if h >= 2:
                    pe.wait_ge(u_copied, h - 1)
                stationary(T0, 2 * p + 1, r, bank[2 + p][:, 0:SEQ], hT_hi, hT_lo)
                if h == 0:
                    pe.wait_ge(vn_done, NT)
                    pe.wait_ge(sg_in, 16 * 6)
                spatial(h, guard=h >= 1)
                if h >= 2:
                    values(h - 2, (h - 2) // QPK)

            pe.wait_ge(gain_in, 16)
            pe.wait_ge(ones_set, 1)
            for b in range(NB):
                pe.matmul(bank[4 + b][:, :], ones_row[:, :], gain_row[:, b * BLK:(b + 1) * BLK],
                          start=True, stop=True).then_inc(gain_rows, 1)
            pe.wait_ge(misc_in, 16)
            for b in range(NB):
                pe.wait_ge(xn_done, b + 1)
                turn_block(xn, 0, 0, b, ident)

            def v_waits(t, c):
                if (t, c) == (1, 0):
                    for b in range(NB):
                        pe.wait_ge(xn_done, NB + b + 1)
                        turn_block(xn, 4, 1, b, ident)
                pe.wait_ge(hl_done, NB * t + c + 1)
                if (t, c) == (0, 2):
                    pe.wait_ge(pool_lo, 1)

            tokens(0, bank[0:2], hT_hi, hT_lo, waits=v_waits,
                   order=[(0, 0), (0, 1), (1, 0), (1, 1), (0, 2), (1, 2), (0, 3), (1, 3)])
            tokens(1, bank[2:4], hT_hi, hT_lo)
            for c in range(2):
                arrived(T_KV, c)
                hi = w_hi[c][:, :].rearrange("p (k n) -> p k n", n=SEQ)
                lo = w_lo[c][:, :].rearrange("p (k n) -> p k n", n=SEQ)
                for kk in range(8):
                    k = 8 * c + kk
                    for t in range(NT):
                        tt = slice(t * P, (t + 1) * P)
                        last = passes(bank[4 + t][:, 0:SEQ], hT_hi[:, k, tt], hT_lo[:, k, tt], hi[:, kk, :], lo[:, kk, :],
                                      k == 0, k == KD - 1)
                last.then_inc(w_used, 1)
            for g in range(NKV):
                arrived(T_KV, 2 + g)
                stationary(T_KV, 2 + g, 0, bank[6 + g][:, 0:SEQ], hT_hi, hT_lo)
            pe.wait_ge(vg_done, 2 * NT)
            pe.wait_ge(vt_done, NT)
            pe.wait_ge(rope_copied, NKV)
            for h in range(NH):
                head(h, T_QU)

            def branches(T0, j, r, p, guard):
                arrived(T0, j, r)
                if guard is not None:
                    pe.wait_ge(gated, guard)
                stationary(T0, j, r, bank[4 + 2 * p][:, 0:SEQ], aT_hi, aT_lo, ks=range(0, 8), done=False)
                stationary(T0, j, r, bank[5 + 2 * p][:, 0:SEQ], bT_hi, bT_lo, ks=range(8, 16))

            def pair(T0, j0, r, n, first=False):
                for g in range(4):
                    arrived(T0, j0 + g, r)
                    if not first:
                        pe.wait_ge(sig_done, 2 * n + g - 3)
                    else:
                        if g == 0:
                            pe.wait_ge(rope_copied, NKV + NH)
                            pe.wait_ge(u_copied, NG)
                    stationary(T0, j0 + g, r, bank[g][:, 0:SEQ], hT_hi, hT_lo)
                    if first and g == 0:
                        scores(NH - 1, 1)
                        turn_probs(NH - 2, 0)
                    if first and g == 1:
                        values(NH - 2, 1)
                        turn_probs(NH - 1, 1)
                    if first and g == 2:
                        values(NH - 1, 1)
                if first:
                    pe.wait_ge(bl_free, NH + 1)
                    pe.wait_ge(al_done, 1)
                for p in range(2):
                    branches(T0, j0 + 4 + p, r, p, None if first else 2 * (n + p) - 2)

            pair(T_MG, 0, 0, 0, first=True)
            pair(T_MG, 6, 0, 2)
            with pe.Fori(1, KD // 4) as i:
                pair(T_MG, 0, 3 * i, 4 * i)
                pair(T_MG, 6, 3 * i, 4 * i + 2)

            for b in range(NB):
                def o_waits(t, c):
                    if b == 0 and t == 0:
                        if c == 0:
                            pe.wait_ge(sig_done, 2 * KD)
                        pe.wait_ge(ml_done, 4 * c + 4)
                    if b >= 2 and c == 0:
                        pe.wait_ge(o_copied, 2 * (b - 2) + t + 1)
                tokens(T_OUT + b, bank[2 * (b % 2):2 * (b % 2) + 2], mT_hi, mT_lo, waits=o_waits, ready=o_ready)
            for t in range(NT):
                pe.wait_ge(diag_done, t + 1)
                for b in range(NB):
                    if b < 2:
                        pe.wait_ge(xg_pool, 2 * t + b + 1)
                    else:
                        pe.wait_ge(xg_dve, 2 * t + b - 1)
                    turn_block(o_tok, 4 * (1 - t), t, b, diag[t])

            def down(T1, j, h, first_bank, tiles):
                slot = j % RING
                if 0 in tiles:
                    arrived(T1, j)
                    pe.wait_ge(act_done, HALF * h + 2 * j + 2)
                hi = w_hi[slot][:, :].rearrange("p (k c n) -> p k c n", k=2, c=2)
                lo = w_lo[slot][:, :].rearrange("p (k c n) -> p k c n", k=2, c=2)
                for kk in range(2):
                    k = 2 * j + kk
                    first, final = k == 0, k == HALF - 1
                    for t in tiles:
                        tt = slice(t * P, (t + 1) * P)
                        dst = [bank[first_bank + 2 * t + c][:, :] for c in range(2)]
                        for c in range(2):
                            pe.matmul(dst[c], act_hi[:, k, tt], hi[:, kk, c, :], start=first, stop=False)
                        for c in range(2):
                            pe.matmul(dst[c], act_hi[:, k, tt], lo[:, kk, c, :], start=False, stop=False)
                        for c in range(2):
                            last = pe.matmul(dst[c], act_lo[:, k, tt], hi[:, kk, c, :], start=False, stop=final)
                if NT - 1 in tiles:
                    last.then_inc(w_used, counts_for(T1 + j // RING, slot))
                return last

            for h in range(2):
                T0 = T_FFN + h * HALF_TURNS
                if h == 1:
                    pe.wait_ge(f_done, 4)
                with pe.Fori(0, UP_TURNS) as i:
                    for j in range(RING):
                        arrived(T0, j, i)
                        pe.wait_ge(c_done, (i + UP_TURNS * h) * RING + j + 1)
                        stationary(T0, j, i, bank[4 * h + j][:, 0:SEQ], hT_hi, hT_lo,
                                   turned=NB * (2 * NT - 1) if (h, j) == (0, 0) else 0)
                for n in range(2):
                    T1 = T0 + UP_TURNS + n * DOWN_TURNS
                    first_bank = down_bank(h, n)
                    if n == 0 and h == 1:
                        pe.wait_ge(f_done, 8)
                    if n == 1:
                        pe.wait_ge(c_done, START_FREE + 2 * HALF * (h + 1))
                    split = DOWN_UNITS - RING if (h, n) == (1, 1) else DOWN_UNITS
                    for j in range(split):
                        down(T1, j, h, first_bank, range(NT))
                    if split < DOWN_UNITS:
                        for t in range(NT):
                            for j in range(split, DOWN_UNITS):
                                last = down(T1, j, h, first_bank, [t])
                            if t == 0:
                                last.then_inc(f_ready, 1)


def _constants():
    import numpy as np
    ident = np.eye(P, dtype=np.float32)
    q = np.arange(P)[:, None, None] + P * np.arange(NT)[None, :, None]
    k = np.arange(SEQ)[None, None, :]
    mask = np.where(np.abs(k - q) <= P, 0.0, MASK_VALUE).astype(np.float32)
    pos = np.arange(SEQ, dtype=np.float32)
    inv = np.float32(ROPE_THETA) ** (-np.arange(0, ROT, 2, dtype=np.float32) / np.float32(ROT))
    ang = (pos[None, :] * inv[:, None]).astype(np.float32)
    cos, sin = np.cos(ang).astype(np.float32), np.sin(ang).astype(np.float32)
    rope = np.stack([np.concatenate([cos, cos]), np.concatenate([-sin, sin])], axis=1)
    return ident, mask, np.ascontiguousarray(rope)


def _pack(w_in, w_a, w_b, w_out, w_up, w_down):
    import numpy as np
    units = []

    def rows(w, k0, nk, c0, nc_):
        return w[k0 * P:(k0 + nk) * P, c0:c0 + nc_].reshape(nk, P, nc_).transpose(1, 0, 2)

    def add(*parts):
        units.append(np.concatenate([p.reshape(P, -1) for p in parts], axis=1))

    u0, v0, q0 = 0, SGW, 2 * SGW
    k0 = q0 + NH * P
    vv0 = k0 + NKV * P
    g0 = vv0 + NKV * P
    for b in range(SGW // BLK):
        for c in range(4):
            add(rows(w_in, 4 * c, 4, v0 + b * BLK, BLK))
    for c in range(2):
        add(rows(w_in, 8 * c, 8, vv0, NKV * P))
    for g in range(NKV):
        add(rows(w_in, 0, KD, k0 + g * P, P))
    for h in range(NH):
        add(rows(w_in, 0, KD, q0 + h * P, P))
        add(rows(w_in, 0, KD, u0 + h * P, P))
    for n0 in range(0, KD, 2):
        for n in (n0, n0 + 1):
            add(rows(w_in, 0, KD, g0 + n * P, P))
            add(rows(w_in, 0, KD, g0 + D + n * P, P))
        for n in (n0, n0 + 1):
            add(rows(w_a, 0, 8, n * P, P), rows(w_b, 0, 8, n * P, P))
    for b in range(NB):
        for c in range(4):
            add(rows(w_out, 4 * c, 4, b * BLK, BLK))
    for h in range(2):
        for i in range(HALF * h, HALF * (h + 1)):
            add(rows(w_up, 0, KD, i * P, P))
            add(rows(w_up, 0, KD, DFF + i * P, P))
        for n in range(2):
            for j in range(DOWN_UNITS):
                add(rows(w_down, HALF * h + 2 * j, 2, n * 1024, 1024))
    return np.stack(units)


def kernel(x, norm_mix_pre, w_in, sg_ln_g, sg_ln_b, sg_w, sg_b, attn_sink, w_branch_a, w_branch_b, w_out,
           norm_mix_post, norm_ffn_pre, w_up, conv_w, conv_b, w_down, norm_ffn_post):
    import numpy as np
    import concourse.bacc as bacc
    from concourse.bass_utils import run_bass_kernel_spmd as run

    a = {k: np.asarray(v) for k, v in dict(
        x=x, npre=norm_mix_pre, w_in=w_in, lg=sg_ln_g, lb=sg_ln_b, sg_w=sg_w, sg_b=sg_b, sink=attn_sink,
        wa=w_branch_a, wb=w_branch_b, wo=w_out, npost=norm_mix_post, nfpre=norm_ffn_pre, w_up=w_up,
        cw=conv_w, cb=conv_b, wd=w_down, nfpost=norm_ffn_post).items()}
    ident, mask, rope = _constants()
    taps = np.concatenate([a["cw"][0], a["cb"]], axis=0)
    conv = taps.reshape(4, 2, KF, P).transpose(3, 2, 1, 0)
    arrays = {
        "x": a["x"].reshape(NT, P, D),
        "weights": _pack(a["w_in"][0], a["wa"][0], a["wb"][0], a["wo"][0], a["w_up"][0], a["wd"][0]),
        "gains": np.concatenate([a["npre"], a["npost"], a["nfpre"], a["nfpost"]], axis=0),
        "sg_gb": np.concatenate([a["lg"], a["lb"]], axis=0),
        "sg_wT": a["sg_w"][0].transpose(2, 0, 1),
        "sg_b": a["sg_b"].reshape(1, NG, P),
        "sink": a["sink"].reshape(1, NH),
        "conv": conv,
        "ident": ident, "mask": mask, "rope": rope,
    }
    arrays = {k: np.ascontiguousarray(v) for k, v in arrays.items()}
    nc = bacc.Bacc("TRN2", target_bir_lowering=False, num_devices=1, dynamic_dma_scratch_size=1024)
    args = [nc.dram_tensor(k, v.shape, mybir.dt.from_np(v.dtype), kind="ExternalInput").ap() for k, v in arrays.items()]
    out = nc.dram_tensor("out", (NT, P, D), mybir.dt.float32, kind="ExternalOutput").ap()
    build(nc, *args, out)
    r = run(nc, [arrays], core_ids=[0])
    return r.results[0]["out"].reshape(1, SEQ, D)
```

```python
import concourse.bass as bass
from concourse import mybir

P = 128
D = 2048
SEQ = 256
NT = SEQ // P
KD = D // P
SGW = 1024
NG = SGW // P
NH = 8
NKV = 2
QPK = NH // NKV
DFF = 5632
KF = DFF // P
HALF = KF // 2
ROT = 32
ROPE_THETA = 500000.0
EPS = 1e-6
MASK_VALUE = -1e30
SCALE = float(P) ** -0.5
UNIT = 2048
RING = 4
BLK = 512
NB = D // BLK

T_V, T_KV, T_QU, T_MG, T_OUT, T_FFN = 0, 2, 3, 7, 19, 23
UP_TURNS = KF * 2 // 2 // RING
DOWN_UNITS = HALF // 2
DOWN_TURNS = -(-DOWN_UNITS // RING)
HALF_TURNS = UP_TURNS + 2 * DOWN_TURNS
T_END = T_FFN + 2 * HALF_TURNS
DOWN_STARTS = [T_FFN + UP_TURNS + h * HALF_TURNS + n * DOWN_TURNS for h in range(2) for n in range(2)]
SHORT_TURNS = [t + DOWN_TURNS - 1 for t in DOWN_STARTS]


def skipped(turn):
    return sum(t < turn for t in SHORT_TURNS)


def exists(turn, slot):
    return turn < T_END and not (slot == RING - 1 and turn in SHORT_TURNS)


def counts_for(turn, slot):
    return 1 if exists(turn, slot + 1) or slot == RING - 1 else 2


def build(nc, x, weights, gains, sg_gb, sg_wT, sg_b, sink, conv, ident_in, mask_in, rope_in, out):
    F32, F32R = mybir.dt.float32, mybir.dt.float32r
    ALU, ACT, AX = mybir.AluOpType, mybir.ActivationFunctionType, mybir.AxisListType

    KB = 1024
    base = 1152
    at = {}

    def region(name, size):
        at[name] = region.top
        region.top += size
    region.top = base
    region("w_hi", RING * 8 * KB)
    region("w_lo", RING * 8 * KB)
    region("raw", RING * 8 * KB)
    region("hT", 32 * KB)
    region("A", 32 * KB)
    region("B", 44 * KB)
    region("gain", 8 * KB)
    region("tmp", 8 * KB)
    region("misc", 2 * KB + 256)

    def sb(name, where, off, shape, dt=F32):
        return nc.alloc_sbuf_tensor_at(name, shape, dt, offset=at[where] + off)

    w_hi = [sb(f"w_hi{s}", "w_hi", s * 8 * KB, [P, UNIT], F32R) for s in range(RING)]
    w_lo = [sb(f"w_lo{s}", "w_lo", s * 8 * KB, [P, UNIT], F32R) for s in range(RING)]
    raw = [sb(f"raw{s}", "raw", s * 8 * KB, [P, UNIT]) for s in range(RING)]
    hT = sb("hT", "hT", 0, [P, 2, KD, SEQ], F32R)
    hT_hi, hT_lo = hT[:, 0], hT[:, 1]
    xn = sb("xn", "A", 0, [P, NT, D])
    x_tok = sb("x_tok", "A", 16 * KB, [P, NT, D])
    aT = sb("aT", "A", 0, [P, 2, NG, SEQ], F32R)
    bT = sb("bT", "A", 16 * KB, [P, 2, NH, SEQ], F32R)
    aT_hi, aT_lo, bT_hi, bT_lo = aT[:, 0], aT[:, 1], bT[:, 0], bT[:, 1]
    o_tok = sb("o_tok", "A", 0, [P, NT, D])
    f_tok = sb("f_tok", "A", 0, [P, NT, D])
    vg = sb("vg", "B", 0, [P, NT, SGW])
    uT = sb("uT", "B", 8 * KB, [P, NG, SEQ])
    vzT = sb("vzT", "B", 16 * KB, [P, NG, SEQ])
    ln_g = sb("ln_g", "B", 24 * KB, [P, SGW])
    ln_b = sb("ln_b", "B", 28 * KB, [P, SGW])
    sgb = sb("sgb", "B", 32 * KB, [P, NG, P])
    sgw = sb("sgw", "B", 36 * KB, [P, NG, P])
    v_tok = sb("v_tok", "B", 40 * KB, [P, NT, NKV * P])
    kT = sb("kT", "B", 42 * KB, [P, NKV, SEQ])
    mT_hi = sb("mT_hi", "B", 0, [P, KD, SEQ], F32R)
    mT_lo = sb("mT_lo", "B", 16 * KB, [P, KD, SEQ], F32R)
    g_ffn = sb("g_ffn", "B", 32 * KB, [P, D])
    act_hi = sb("act_hi", "B", 0, [P, HALF, SEQ], F32R)
    act_lo = sb("act_lo", "B", 22 * KB, [P, HALF, SEQ], F32R)
    gain = sb("gain", "gain", 0, [P, D])
    prob = [sb(f"prob{i}", "tmp", i * 2 * KB, [P, NT, SEQ]) for i in range(2)]
    pT = sb("pT", "tmp", 4 * KB, [P, NT, SEQ])
    qT = [sb(f"qT{i}", "tmp", (6 + i) * KB, [P, SEQ]) for i in range(2)]
    sig = [[sb(f"sig{p}{i}", "tmp", (2 * p + i) * KB, [P, SEQ]) for i in range(2)] for p in range(2)]
    ab = [[sb(f"ab{p}{i}", "tmp", (4 + 2 * p + i) * KB, [P, SEQ]) for i in range(2)] for p in range(2)]
    squares = sb("squares", "tmp", 0, [P, BLK])
    diag = [sb(f"diag{t}", "tmp", 4 * KB + 512 * t, [P, P]) for t in range(NT)]
    conv_o = [[sb(f"conv_o{p}{i}", "tmp", (2 * p + i) * KB, [P, SEQ]) for i in range(2)] for p in range(2)]
    gelu_o = [sb(f"gelu_o{p}", "tmp", (4 + p) * KB, [P, SEQ]) for p in range(2)]
    prod = [sb(f"prod{p}", "tmp", (6 + p) * KB, [P, SEQ]) for p in range(2)]
    up_o = [[sb(f"up_o{p}{i}", "gain", (2 * p + i) * KB, [P, SEQ]) for i in range(2)] for p in range(2)]
    ident = sb("ident", "misc", 0, [P, P])
    convw = sb("convw", "misc", 512, [P, KF, 2, 4])
    small = sb("small", "misc", 512 + 1408, [P, 64])
    mask = sb("mask", "gain", 0, [P, NT, SEQ])
    ropes = sb("ropes", "gain", 2 * KB, [ROT, 2, SEQ])
    rot = sb("rot", "gain", 4 * KB, [ROT, SEQ])

    ssq, msq, rstd = small[:, 0:2], small[:, 2:4], small[:, 4:6]
    ssq4 = small[:, 6:14]
    neg_half = small[:, 14:15]
    mean_var = [small[:, 16 + 2 * t:18 + 2 * t] for t in range(NT)]
    stats = [small[:, 20 + 12 * t:32 + 12 * t] for t in range(NT)]
    gain_row = sb("gain_row", "tmp", 0, [1, D])
    ones_row = sb("ones_row", "gain", 5 * KB, [1, P])
    smax, negm, psum_p, esink = (small[:, 44 + 2 * i:46 + 2 * i] for i in range(4))
    den, rden = small[:, 52:54], small[:, 54:56]
    sinks = small[:, 56:64]

    def one(tensor, n):
        return tensor[:, bass.ds(n, 1), :].rearrange("p o s -> p (o s)")

    bank = [nc.alloc_psum_tensor(f"bank{i}", [P, BLK], F32) for i in range(8)]

    def sem(name):
        return nc.alloc_semaphore(name)

    raw_ready = [sem(f"raw_ready{s}") for s in range(RING)]
    wh_ready, wl_ready, w_used = sem("wh_ready"), sem("wl_ready"), sem("w_used")
    x_in = [[sem(f"x_in{t}{c}") for c in range(2)] for t in range(NT)]
    gain_rows, pool_lo = sem("gain_rows"), sem("pool_lo")
    ones_set, gain_in, misc_in, tables_in, sg_in = sem("ones_set"), sem("gain_in"), sem("misc_in"), sem("tables_in"), sem("sg_in")
    post_in, ffn_gain_in, x_again, last_gain_in = sem("post_in"), sem("ffn_gain_in"), sem("x_again"), sem("last_gain_in")
    half_set = sem("half_set")
    sq_done, red_done, ms_done, rstd_done = (sem(n) for n in ("sq_done", "red_done", "ms_done", "rstd_done"))
    xn_done, tr_done, hh_done, hl_done = sem("xn_done"), sem("tr_done"), sem("hh_done"), sem("hl_done")
    vg_done, st_done, mv_done = sem("vg_done"), sem("st_done"), sem("mv_done")
    vhat_done, vmul_done, vn_done = sem("vhat_done"), sem("vmul_done"), sem("vn_done")
    vt_done = sem("vt_done")
    qk_summed, rope_turned, rope_sin, rope_cos, rope_done = (
        sem(n) for n in ("qk_summed", "rope_turned", "rope_sin", "rope_cos", "rope_done"))
    qk_lo, u_lo = sem("qk_lo"), sem("u_lo")
    u_summed, vz_ready, vz_done = sem("u_summed"), sem("vz_ready"), sem("vz_done")
    sc_ready, sc_read, mx_done, nm_done, exp_done = (
        sem(n) for n in ("sc_ready", "sc_read", "mx_done", "nm_done", "exp_done"))
    den_done, rden_done, p_ready = sem("den_done"), sem("rden_done"), sem("p_ready")
    pt_ready, pt_free, pv_ready, bh_done, bl_free = (
        sem(n) for n in ("pt_ready", "pt_free", "pv_ready", "bh_done", "bl_free"))
    ug_done, a_done, ah_done, al_done = sem("ug_done"), sem("a_done"), sem("ah_done"), sem("al_done")
    gate_lo, gate_sum, ab_lo, ab_sum = (sem(n) for n in ("gate_lo", "gate_sum", "ab_lo", "ab_sum"))
    sig_done, gated, m_done, mh_done, ml_done = (
        sem(n) for n in ("sig_done", "gated", "m_done", "mh_done", "ml_done"))
    o_ready, o_copied, o_sq = sem("o_ready"), sem("o_copied"), sem("o_sq")
    x1_done, x1_sq, xg_pool, xg_dve, diag_done = (
        sem(n) for n in ("x1_done", "x1_sq", "xg_pool", "xg_dve", "diag_done"))
    up_lo, up_free = sem("up_lo"), sem("up_free")
    c_mid, c_left, c_done, ge_done, pr_done, acth_done, act_done = (
        sem(n) for n in ("c_mid", "c_left", "c_done", "ge_done", "pr_done", "acth_done", "act_done"))
    f_ready, f_done, f_sq, fg_pool, fg_dve, y_done = (
        sem(n) for n in ("f_ready", "f_done", "f_sq", "fg_pool", "fg_dve", "y_done"))
    stored = sem("stored")

    N_PRE, N_V, N_POST, N_FFN, N_LAST = [0, 1], [2, 3], [4, 6], [5, 7], [8, 9]
    V_Q = RING * T_QU
    START_FREE = RING

    def down_bank(h, n):
        return 4 * (1 - h) if n == 0 else 4 * h

    def load_unit(sp, T0, j, r=0):
        turn, slot = T0 + j // RING, j % RING
        if not exists(turn, slot):
            return
        if turn > 0:
            sp.wait_ge(wl_ready, (turn + r) * RING + slot - RING + 1)
        sp.dma_start(raw[slot][:, :], weights[(turn + r) * RING + slot - skipped(turn)]).then_inc(raw_ready[slot], 16)

    def round_unit(act, T0, j, r=0):
        turn, slot = T0 + j // RING, j % RING
        if not exists(turn, slot):
            return
        v = (turn + r) * RING + slot
        act.wait_ge(raw_ready[slot], (turn + r + 1 - (skipped(turn) if slot == RING - 1 else 0)) * 16)
        if turn > 0:
            act.wait_ge(w_used, v - RING + 1)
        act.activation(w_hi[slot][:, :], raw[slot][:, :], ACT.Copy).then_inc(wh_ready, counts_for(turn, slot))

    def rest_unit(dve, T0, j, r=0):
        turn, slot = T0 + j // RING, j % RING
        if not exists(turn, slot):
            return
        dve.wait_ge(wh_ready, (turn + r) * RING + slot + 1)
        count = 2 if (turn, slot) == (0, 3) else counts_for(turn, slot)
        dve.tensor_tensor(w_lo[slot][:, :], raw[slot][:, :], w_hi[slot][:, :], ALU.subtract).then_inc(wl_ready, count)

    block = nc.Block()
    with block:
        @block.sync
        def _(sp):
            half = D // 2
            sp.dma_start(gain_row[:, :], gains[0:1, :]).then_inc(gain_in, 16)
            for c in range(2):
                sp.dma_start(x_tok[:, 0, c * half:(c + 1) * half], x[0][:, c * half:(c + 1) * half]).then_inc(x_in[0][c], 16)
            load_unit(sp, 0, 0)
            load_unit(sp, 0, 1)
            for c in range(2):
                sp.dma_start(x_tok[:, 1, c * half:(c + 1) * half], x[1][:, c * half:(c + 1) * half]).then_inc(x_in[1][c], 16)
            load_unit(sp, 0, 2)
            load_unit(sp, 0, 3)
            sp.dma_start(ln_g[:, :], sg_gb[0:1, :].partition_broadcast(P)).then_inc(sg_in, 16)
            sp.dma_start(ln_b[:, :], sg_gb[1:2, :].partition_broadcast(P)).then_inc(sg_in, 16)
            sp.dma_start(sgb[:, :, :], sg_b.partition_broadcast(P)).then_inc(sg_in, 16)
            sp.dma_start(sgw[:, :, :], sg_wT).then_inc(sg_in, 16)
            sp.dma_start(sinks, sink.partition_broadcast(P)).then_inc(sg_in, 16)
            sp.dma_start(convw[:, :, :, :], conv).then_inc(sg_in, 16)
            for j in range(RING):
                if j == 2:
                    sp.wait_ge(pool_lo, 1)
                load_unit(sp, 1, j)
            sp.dma_start(mask[:, :, :], mask_in).then_inc(tables_in, 16)
            sp.dma_start(ropes[:, :, :], rope_in).then_inc(tables_in, 16)
            with sp.Fori(0, T_MG + 4 - 2) as i:
                for j in range(RING):
                    load_unit(sp, 2, j, i)
            sp.wait_ge(sc_read, NH)
            sp.wait_ge(rope_done, NKV + NH)
            sp.dma_start(gain[:, :], gains[1:2, :].partition_broadcast(P)).then_inc(post_in, 16)
            with sp.Fori(0, T_OUT + 2 - (T_MG + 4)) as i:
                for j in range(RING):
                    load_unit(sp, T_MG + 4, j, i)
            sp.wait_ge(w_used, RING * T_OUT)
            for t in range(NT):
                sp.dma_start(x_tok[:, t, :], x[t]).then_inc(x_again, 16)
            sp.dma_start(g_ffn[:, :], gains[2:3, :].partition_broadcast(P)).then_inc(ffn_gain_in, 16)
            with sp.Fori(0, T_FFN - (T_OUT + 2)) as i:
                for j in range(RING):
                    load_unit(sp, T_OUT + 2, j, i)
            for h in range(2):
                T0 = T_FFN + h * HALF_TURNS
                with sp.Fori(0, UP_TURNS) as i:
                    for j in range(RING):
                        load_unit(sp, T0, j, i)
                for n in range(2):
                    if (h, n) == (1, 1):
                        sp.wait_ge(c_done, 2 * KF)
                        sp.dma_start(gain[:, :], gains[3:4, :].partition_broadcast(P)).then_inc(last_gain_in, 16)
                    for j in range(DOWN_TURNS * RING):
                        load_unit(sp, T0 + UP_TURNS + n * DOWN_TURNS, j)
            for t in range(NT):
                for b in range(NB):
                    col = slice(b * BLK, (b + 1) * BLK)
                    sp.wait_ge(y_done, NB * t + b + 1)
                    sp.dma_start(out[t][:, col], f_tok[:, t, col]).then_inc(stored, 16)
            sp.wait_ge(stored, 16 * NT * NB)

        @block.gpsimd
        def _(pool):
            pool.memset(ones_row[:, :], 1.0).then_inc(ones_set, 1)
            pool.memset(neg_half, -0.5).then_inc(half_set, 1)
            pool.wait_ge(half_set, 1)

            def power(n, t):
                pool.wait_ge(ms_done, n[t] + 1)
                pool.tensor_tensor(rstd[:, t:t + 1], msq[:, t:t + 1], neg_half, ALU.pow).then_inc(rstd_done, 1)

            def rope(n, dst, ahead=0):
                c = n + 1 + ahead
                pool.wait_ge(rope_turned, c)
                pool.tensor_tensor(rot[:, :], rot[:, :], ropes[:, 1, :], ALU.mult).then_inc(rope_sin, 1)
                pool.tensor_tensor(dst, dst, ropes[:, 0, :], ALU.mult).then_inc(rope_cos, 1)
                pool.wait_ge(rope_sin, c)
                pool.wait_ge(rope_cos, c)
                pool.tensor_tensor(dst, dst, rot[:, :], ALU.add).then_inc(rope_done, 1)

            power(N_PRE, 0)
            power(N_PRE, 1)
            pool.wait_ge(wh_ready, 3)
            pool.tensor_tensor(w_lo[2][:, :], raw[2][:, :], w_hi[2][:, :], ALU.subtract).then_inc(pool_lo, 1)
            pool.wait_ge(sg_in, 16 * 6)
            for t in range(NT):
                power(N_V, t)
                pool.wait_ge(vhat_done, t + 1)
                pool.tensor_tensor(vg[:, t, :], vg[:, t, :], ln_g[:, :], ALU.mult).then_inc(vmul_done, 1)
                pool.wait_ge(vmul_done, t + 1)
                pool.tensor_tensor(vg[:, t, :], vg[:, t, :], ln_b[:, :], ALU.add).then_inc(vn_done, 1)
            pool.wait_ge(tables_in, 32)
            for g in range(NKV):
                rope(g, kT[0:ROT, g, :])
            with pool.Fori(0, NH // 2) as i:
                for p in range(2):
                    rope(NKV + p, qT[p][0:ROT, :], 2 * i)
            pool.wait_ge(ffn_gain_in, 16)
            for t in range(NT):
                power(N_POST, t)
                for b in range(2):
                    col = slice(b * BLK, (b + 1) * BLK)
                    pool.wait_ge(x1_done, NB * t + b + 1)
                    pool.tensor_tensor(o_tok[:, t, col], x_tok[:, t, col], g_ffn[:, col], ALU.mult).then_inc(xg_pool, 1)
                power(N_FFN, t)
            pool.wait_ge(last_gain_in, 16)
            for t in range(NT):
                for b in range(2):
                    col = slice(b * BLK, (b + 1) * BLK)
                    pool.wait_ge(f_sq, 2 * t + b + 1)
                    pool.tensor_tensor(f_tok[:, t, col], f_tok[:, t, col], gain[:, col], ALU.mult).then_inc(fg_pool, 1)
            for t in range(NT):
                power(N_LAST, t)

        @block.scalar
        def _(act):
            def square(t, b, src, junk, size, done):
                act.activation(junk, src[:, t, b * size:(b + 1) * size], ACT.Square,
                               accum_out=ssq4[:, NB * t + b:NB * t + b + 1]).then_inc(done, 1)

            def turn_hi(first_bank, n, t, blocks=range(NB)):
                for b in blocks:
                    act.wait_ge(tr_done, n + NB * t + b + 1)
                    act.activation(hT_hi[:, 4 * b:4 * b + 4, t * P:(t + 1) * P],
                                   bank[first_bank + b][:, :].rearrange("p (k s) -> p k s", k=4),
                                   ACT.Copy).then_inc(hh_done, 1)

            def low_half(v, b, dst, done):
                act.wait_ge(w_used, v + 1)
                act.activation(dst, bank[b][:, SEQ:2 * SEQ], ACT.Copy).then_inc(done, 1)

            def exps(h, p):
                act.wait_ge(nm_done, h + 1)
                for t in range(NT):
                    act.activation(prob[p][:, t, :], prob[p][:, t, :], ACT.Exp, bias=negm[:, t:t + 1],
                                   accum_out=psum_p[:, t:t + 1]).then_inc(exp_done, 1)
                act.activation(esink, negm, ACT.Exp, bias=sinks[:, bass.ds(h, 1)]).then_inc(exp_done, 1)

            def b_hi(h):
                act.wait_ge(pv_ready, h + 1)
                act.activation(one(bT_hi, h), bank[6][:, 0:SEQ], ACT.Copy).then_inc(bh_done, 1)

            def head(h, p, T0, r, first=False, second=False):
                q = V_Q + 2 * h
                round_unit(act, T0, 2 * p + 3, r)
                if not (first or second):
                    act.wait_ge(sc_ready, h - 1)
                low_half(q, p, qT[p][:, :], qk_lo)
                if not first:
                    exps(h - 1, 1 - p)
                round_unit(act, T0, 2 * p + 4, r)
                low_half(q + 1, 2 + p, one(uT, h), u_lo)
                if not (first or second):
                    b_hi(h - 2)

            act.dma_start(ident[:, :], ident_in).then_inc(misc_in, 16)
            for t in range(NT):
                for c in range(2):
                    act.wait_ge(x_in[t][c], 16)
                    square(t, c, x_tok, xn[:, t, c * D // 2:(c + 1) * D // 2], D // 2, sq_done)
                if t == 0:
                    round_unit(act, 0, 0)
                    turn_hi(0, 0, 0, [0, 1])
                    round_unit(act, 0, 1)
            turn_hi(0, 0, 0, [2, 3])
            round_unit(act, 0, 2)
            turn_hi(4, 0, 1)
            round_unit(act, 0, 3)
            for b in range(2):
                for j in range(RING):
                    if b + j > 0:
                        round_unit(act, b, j + 3)
                act.wait_ge(w_used, RING * (b + 1))
                for t in range(NT):
                    act.activation(vg[:, t, b * BLK:(b + 1) * BLK], bank[2 * b + t][:, :], ACT.Gelu_apprx_tanh).then_inc(vg_done, 1)
            round_unit(act, T_KV, 3)
            round_unit(act, T_KV, 4)
            act.wait_ge(w_used, RING * T_KV + 2)
            for t in range(NT):
                act.activation(v_tok[:, t, :], bank[4 + t][:, 0:SEQ], ACT.Copy).then_inc(vt_done, 1)
            for g in range(NKV):
                round_unit(act, T_KV, 5 + g)
                low_half(RING * T_KV + 2 + g, 6 + g, kT[:, g, :], qk_lo)
            act.wait_ge(sg_in, 16 * 6)
            head(0, 0, T_QU, 0, first=True)
            head(1, 1, T_QU, 0, second=True)
            with act.Fori(1, NH // 2) as i:
                for p in range(2):
                    head(2 * i + p, p, T_QU, i)

            def sigmoid(n, i, p, v, guard=True):
                act.wait_ge(w_used, v + 1)
                if guard:
                    act.wait_ge(ml_done, n - 1)
                act.activation(sig[p][i][:, :], bank[2 * p + i][:, SEQ:2 * SEQ], ACT.Copy).then_inc(gate_lo, 1)
                act.wait_ge(gate_sum, 2 * n + i + 1)
                act.activation(sig[p][i][:, :], sig[p][i][:, :], ACT.Sigmoid).then_inc(sig_done, 1)

            def m_hi(n, p):
                act.wait_ge(m_done, n + 1)
                act.activation(one(mT_hi, n), sig[p][0][:, :], ACT.Copy).then_inc(mh_done, 1)

            def pair(T0, j0, r, n, first=False):
                v = (T0 + r) * RING + j0
                if first:
                    round_unit(act, T0, j0 + 3, r)
                    exps(NH - 1, 1)
                    round_unit(act, T0, j0 + 4, r)
                    act.wait_ge(u_summed, NG)
                    act.activation(uT[:, :, :], uT[:, :, :], ACT.Gelu_apprx_tanh).then_inc(ug_done, 1)
                    b_hi(NH - 2)
                    round_unit(act, T0, j0 + 5, r)
                    act.wait_ge(a_done, 1)
                    act.activation(aT_hi[:, :, :], uT[:, :, :], ACT.Copy).then_inc(ah_done, 1)
                    b_hi(NH - 1)
                    act.wait_ge(pt_ready, NH)
                    for g in range(4):
                        if g == 3:
                            round_unit(act, T0, j0 + 6, r)
                        sigmoid(n + g // 2, g % 2, g // 2, v + g, guard=False)
                else:
                    for g in range(4):
                        round_unit(act, T0, j0 + 3 + g, r)
                        sigmoid(n + g // 2, g % 2, g // 2, v + g)
                for p in range(2):
                    round_unit(act, T0, j0 + 7 + p, r)
                    act.wait_ge(w_used, v + 4 + p + 1)
                    for i in range(2):
                        act.activation(ab[p][i][:, :], bank[4 + 2 * p + i][:, SEQ:2 * SEQ], ACT.Copy).then_inc(ab_lo, 1)
                    m_hi(n + p, p)

            pair(T_MG, 0, 0, 0, first=True)
            pair(T_MG, 6, 0, 2)
            with act.Fori(1, KD // 4) as i:
                pair(T_MG, 0, 3 * i, 4 * i)
                pair(T_MG, 6, 3 * i, 4 * i + 2)

            for b in range(NB):
                round_unit(act, T_OUT + b, 3)
                for t in range(NT):
                    if (b == 0 and t == 0) or (0 < b < NB - 1 and t == 1):
                        round_unit(act, T_OUT + b, 4)
                        round_unit(act, T_OUT + b, 5)
                    if t == 0:
                        act.wait_ge(o_ready, b + 1)
                    else:
                        act.wait_ge(w_used, RING * (T_OUT + b + 1))
                    if b + t > 0:
                        act.wait_ge(o_sq, 2 * b + t)
                    if (b, t) == (NB - 1, 1):
                        act.wait_ge(x1_sq, NB)
                    act.activation(squares[:, :], bank[2 * (b % 2) + t][:, :], ACT.Square,
                                   accum_out=ssq4[:, NB * t + b:NB * t + b + 1]).then_inc(o_sq, 1)
                    if b == NB - 1:
                        act.wait_ge(o_sq, 2 * b + t + 1)
                        for c in range(NB):
                            if t == 0 and c % 2 == 0:
                                round_unit(act, T_OUT + b, 4 + c // 2)
                            act.wait_ge(x1_done, NB * t + c + 1)
                            if c > 0:
                                act.wait_ge(x1_sq, NB * t + c)
                            square(t, c, x_tok, squares[:, :], BLK, x1_sq)
                if b < NB - 1:
                    round_unit(act, T_OUT + b, 6)
            turn_hi(4, NB * NT, 0)
            turn_hi(0, NB * NT, 1)
            round_unit(act, T_OUT + NB - 1, 6)

            act.wait_ge(x1_sq, NB * NT)

            def finish(pp, h, p):
                act.wait_ge(pr_done, pp + 1 + 2)
                act.activation(one(act_hi, pp - HALF * h), prod[p][:, :], ACT.Copy).then_inc(acth_done, 1)

            def up(T0, j0, r, pp, h, first=False):
                p = (j0 // 2) % 2
                v = (T0 + r) * RING + j0
                for i in range(2):
                    round_unit(act, T0, j0 + i + 3, r)
                    act.wait_ge(w_used, v + i + 1)
                    act.activation(up_o[p][i][:, :], bank[4 * h + 2 * p + i][:, SEQ:2 * SEQ], ACT.Copy).then_inc(up_lo, 1)
                    act.wait_ge(up_free, START_FREE + 2 * pp + i + 1)
                    act.wait_ge(pr_done, pp + 1)
                    act.activation(conv_o[p][i][:, :], up_o[p][i][:, :], ACT.Identity,
                                   scale=convw[:, bass.ds(pp, 1), i, 1], bias=convw[:, bass.ds(pp, 1), i, 3]).then_inc(c_mid, 1)
                    if i == 0 and not first:
                        finish(pp - 1, h, 1 - p)
                act.wait_ge(c_done, 2 * pp + 1)
                act.activation(gelu_o[p][:, :], conv_o[p][0][:, :], ACT.Gelu_apprx_tanh).then_inc(ge_done, 1)

            for h in range(2):
                T0 = T_FFN + h * HALF_TURNS
                for q in range(2):
                    up(T0, 2 * q, 0, q + HALF * h, h, first=q == 0)
                with act.Fori(1, UP_TURNS) as i:
                    for q in range(2):
                        up(T0, 2 * q, i, 2 * i + q + HALF * h, h)
                finish(HALF * (h + 1) - 1, h, 1)
                for n in range(2):
                    for j in range(DOWN_TURNS * RING):
                        round_unit(act, T0 + UP_TURNS + n * DOWN_TURNS, j + 3)
            for n in range(2):
                for t in range(NT):
                    for c in range(2):
                        b = 2 * n + c
                        act.wait_ge(f_done, 8 + 4 * n + 2 * t + c + 1)
                        if n + t + c > 0:
                            act.wait_ge(f_sq, 4 * n + 2 * t + c)
                        act.activation(squares[:, :], f_tok[:, t, b * BLK:(b + 1) * BLK], ACT.Square,
                                       accum_out=ssq4[:, NB * t + b:NB * t + b + 1]).then_inc(f_sq, 1)

        @block.vector
        def _(dve):
            def mean_square(t):
                dve.tensor_scalar(msq[:, t:t + 1], ssq[:, t:t + 1], 1.0 / D, EPS, ALU.mult, ALU.add).then_inc(ms_done, 1)

            def mean_square_of(t, parts, count):
                dve.tensor_reduce(ssq[:, t:t + 1], ssq4[:, NB * t:NB * t + parts], AX.X, ALU.add).then_inc(red_done, 1)
                dve.wait_ge(red_done, count)
                mean_square(t)

            def turn_lo(first_bank, n, t, blocks=range(NB)):
                for b in blocks:
                    dst = (slice(None), slice(4 * b, 4 * b + 4), slice(t * P, (t + 1) * P))
                    dve.wait_ge(hh_done, n + NB * t + b + 1)
                    dve.tensor_tensor(hT_lo[dst], bank[first_bank + b][:, :].rearrange("p (k s) -> p k s", k=4),
                                      hT_hi[dst], ALU.subtract).then_inc(hl_done, 1)

            def both_halves(b, dst, low_done, count, done):
                dve.wait_ge(low_done, count)
                dve.tensor_tensor(dst, bank[b][:, 0:SEQ], dst, ALU.add).then_inc(done, 1)

            def turned(n, src):
                dve.wait_ge(qk_summed, n + 1)
                if not isinstance(n, int) or n > 0:
                    dve.wait_ge(rope_done, n)
                dve.stream_shuffle(rot[:, :], src, [(i + ROT // 2) % ROT for i in range(ROT)]).then_inc(rope_turned, 1)

            def scores(h, p, guard=True):
                dve.wait_ge(sc_ready, h + 1)
                if guard:
                    dve.wait_ge(pt_ready, h - 1)
                dve.scalar_tensor_tensor(prob[p][:, :, :], bank[4][:, :].rearrange("p (t s) -> p t s", t=NT), SCALE,
                                         mask[:, :, :], ALU.mult, ALU.add).then_inc(sc_read, 1)
                dve.wait_ge(sc_read, h + 1)
                dve.tensor_reduce(smax, prob[p][:, :, :], AX.X, ALU.max).then_inc(mx_done, 1)
                dve.wait_ge(mx_done, h + 1)
                dve.tensor_scalar(negm, smax, sinks[:, bass.ds(h, 1)], -1.0, ALU.max, ALU.mult).then_inc(nm_done, 1)

            def probabilities(h, p):
                dve.wait_ge(exp_done, 3 * h + 3)
                dve.tensor_tensor(den, psum_p, esink, ALU.add).then_inc(den_done, 1)
                dve.wait_ge(den_done, h + 1)
                dve.reciprocal(rden, den).then_inc(rden_done, 1)
                dve.wait_ge(rden_done, h + 1)
                for t in range(NT):
                    dve.tensor_scalar(prob[p][:, t, :], prob[p][:, t, :], rden[:, t:t + 1], None, ALU.mult).then_inc(p_ready, 1)

            def copy_pT(h, guard=True):
                dve.wait_ge(pt_ready, h + 1)
                if guard:
                    dve.wait_ge(pv_ready, h)
                dve.tensor_copy(pT[:, :, :], bank[5][:, :].rearrange("p (k s) -> p k s", k=NT)).then_inc(pt_free, 1)

            def vz(h):
                dve.wait_ge(vz_ready, h + 1)
                dve.tensor_tensor(vzT[:, bass.ds(h, 1), :].rearrange("p g (c t) -> p (g c) t", c=NT),
                                  bank[7][:, 0:SEQ].rearrange("p (c t) -> p c t", c=NT),
                                  sgb[:, bass.ds(h, 1), :].broadcast_to([P, NT, P]), ALU.add).then_inc(vz_done, 1)

            def b_lo(h):
                dve.wait_ge(bh_done, h + 1)
                dve.tensor_tensor(one(bT_lo, h), bank[6][:, 0:SEQ], one(bT_hi, h), ALU.subtract).then_inc(bl_free, 1)

            def head(h, p, T0, r, first=False, second=False, third=False):
                rest_unit(dve, T0, 2 * p + 3, r)
                both_halves(p, qT[p][:, :], qk_lo, NKV + h + 1, qk_summed)
                turned(NKV + h, qT[p][0:ROT, :])
                if not first:
                    scores(h - 1, 1 - p, guard=not (second or third))
                if not (first or second):
                    copy_pT(h - 2, guard=not third)
                rest_unit(dve, T0, 2 * p + 4, r)
                if not first:
                    probabilities(h - 1, 1 - p)
                both_halves(2 + p, one(uT, h), u_lo, h + 1, u_summed)
                vz(h)
                if not (first or second):
                    b_lo(h - 2)

            def mixer_norm(t):
                dve.wait_ge(sq_done, 2 * t + 2)
                mean_square_of(t, 2, t + 1)

            def mixer_scale(t, b):
                col = slice(b * BLK, (b + 1) * BLK)
                dve.scalar_tensor_tensor(xn[:, t, col], x_tok[:, t, col], rstd[:, t:t + 1], bank[4 + b][:, :],
                                         ALU.mult, ALU.mult).then_inc(xn_done, 1)

            mixer_norm(0)
            dve.wait_ge(rstd_done, 1)
            for b in range(NB):
                dve.wait_ge(gain_rows, b + 1)
                mixer_scale(0, b)
            rest_unit(dve, 0, 0)
            turn_lo(0, 0, 0, [0, 1])
            rest_unit(dve, 0, 1)
            mixer_norm(1)
            dve.wait_ge(rstd_done, 2)
            for b in range(NB):
                mixer_scale(1, b)
            turn_lo(0, 0, 0, [2, 3])
            turn_lo(4, 0, 1)
            rest_unit(dve, 0, 3)
            for b in range(2):
                for j in range(RING):
                    if b + j > 0:
                        rest_unit(dve, b, j + 3)
                for t in range(NT):
                    dve.wait_ge(vg_done, NT * b + t + 1)
                    dve.bn_stats(stats[t][:, 6 * b:6 * b + 6], vg[:, t, b * BLK:(b + 1) * BLK]).then_inc(st_done, 1)
            rest_unit(dve, T_KV, 3)
            for t in range(NT):
                dve.wait_ge(st_done, 3 + t)
                dve.bn_aggr(mean_var[t], stats[t]).then_inc(mv_done, 1)
                dve.wait_ge(mv_done, t + 1)
                dve.tensor_scalar(msq[:, t:t + 1], mean_var[t][:, 1:2], EPS, None, ALU.add).then_inc(ms_done, 1)
            for t in range(NT):
                dve.wait_ge(rstd_done, N_V[t] + 1)
                dve.tensor_scalar(vg[:, t, :], vg[:, t, :], mean_var[t][:, 0:1], rstd[:, t:t + 1],
                                  ALU.subtract, ALU.mult).then_inc(vhat_done, 1)
            rest_unit(dve, T_KV, 4)
            for g in range(NKV):
                rest_unit(dve, T_KV, 5 + g)
                both_halves(6 + g, kT[:, g, :], qk_lo, g + 1, qk_summed)
                turned(g, kT[0:ROT, g, :])
            dve.wait_ge(tables_in, 32)
            dve.wait_ge(sg_in, 16 * 6)
            dve.sem_inc(pt_free, 1)
            dve.sem_inc(bl_free, 1)
            for h in range(NH):
                head(h, h % 2, T_QU + h // 2, 0, first=h == 0, second=h == 1, third=h == 2)

            def gate(n, i, p):
                both_halves(2 * p + i, sig[p][i][:, :], gate_lo, 2 * n + i + 1, gate_sum)

            def merged(n, p):
                for i in range(2):
                    both_halves(4 + 2 * p + i, ab[p][i][:, :], ab_lo, 2 * n + i + 1, ab_sum)
                dve.wait_ge(sig_done, 2 * n + 2)
                dve.wait_ge(ab_sum, 2 * n + 2)
                for i in range(2):
                    dve.tensor_tensor(sig[p][i][:, :], sig[p][i][:, :], ab[p][i][:, :], ALU.mult).then_inc(gated, 1)
                dve.wait_ge(gated, 2 * n + 2)
                dve.tensor_tensor(sig[p][0][:, :], sig[p][0][:, :], sig[p][1][:, :], ALU.add).then_inc(m_done, 1)
                dve.wait_ge(mh_done, n + 1)
                dve.tensor_tensor(one(mT_lo, n), sig[p][0][:, :], one(mT_hi, n), ALU.subtract).then_inc(ml_done, 1)

            def pair(T0, j0, r, n, first=False):
                if first:
                    rest_unit(dve, T0, j0 + 3, r)
                    scores(NH - 1, 1)
                    copy_pT(NH - 2)
                    probabilities(NH - 1, 1)
                    rest_unit(dve, T0, j0 + 4, r)
                    b_lo(NH - 2)
                    copy_pT(NH - 1)
                    dve.wait_ge(ug_done, 1)
                    dve.wait_ge(vz_done, NG)
                    dve.tensor_tensor(uT[:, :, :], uT[:, :, :], vzT[:, :, :], ALU.mult).then_inc(a_done, 1)
                    rest_unit(dve, T0, j0 + 5, r)
                    dve.wait_ge(ah_done, 1)
                    dve.tensor_tensor(aT_lo[:, :, :], uT[:, :, :], aT_hi[:, :, :], ALU.subtract).then_inc(al_done, 1)
                    b_lo(NH - 1)
                    for g in range(4):
                        if g == 3:
                            rest_unit(dve, T0, j0 + 6, r)
                        gate(n + g // 2, g % 2, g // 2)
                else:
                    for g in range(4):
                        gate(n + g // 2, g % 2, g // 2)
                        rest_unit(dve, T0, j0 + 3 + g, r)
                for p in range(2):
                    merged(n + p, p)
                    rest_unit(dve, T0, j0 + 7 + p, r)

            pair(T_MG, 0, 0, 0, first=True)
            pair(T_MG, 6, 0, 2)
            with dve.Fori(1, KD // 4) as i:
                pair(T_MG, 0, 3 * i, 4 * i)
                pair(T_MG, 6, 3 * i, 4 * i + 2)

            def scaled(t, b):
                col = slice(b * BLK, (b + 1) * BLK)
                dve.wait_ge(x1_done, NB * t + b + 1)
                dve.tensor_tensor(o_tok[:, t, col], x_tok[:, t, col], g_ffn[:, col], ALU.mult).then_inc(xg_dve, 1)

            def residual(t):
                dve.wait_ge(x_again, 16 * NT)
                dve.wait_ge(rstd_done, N_POST[t] + 1)
                dve.wait_ge(o_copied, 2 * (NB - 1) + t + 1)
                for b in range(NB):
                    col = slice(b * BLK, (b + 1) * BLK)
                    dve.scalar_tensor_tensor(x_tok[:, t, col], o_tok[:, t, col], rstd[:, t:t + 1], x_tok[:, t, col],
                                             ALU.mult, ALU.add).then_inc(x1_done, 1)
                dve.wait_ge(ffn_gain_in, 16)
                scaled(t, 2)
                if t == 0:
                    scaled(t, 3)
                    rest_unit(dve, T_OUT + NB - 1, 4)
                    rest_unit(dve, T_OUT + NB - 1, 5)
                dve.wait_ge(x1_sq, NB * (t + 1))
                mean_square_of(t, NB, NT + 2 * t + 2)
                if t == 1:
                    scaled(t, 3)

            def diagonal(t):
                dve.wait_ge(rstd_done, N_FFN[t] + 1)
                dve.tensor_scalar(diag[t][:, :], ident[:, :], rstd[:, t:t + 1], None, ALU.mult).then_inc(diag_done, 1)

            dve.wait_ge(post_in, 16)
            for b in range(NB):
                rest_unit(dve, T_OUT + b, 3)
                for t in range(NT):
                    if (b == 0 and t == 0) or (0 < b < NB - 1 and t == 1):
                        rest_unit(dve, T_OUT + b, 4)
                        rest_unit(dve, T_OUT + b, 5)
                    dve.wait_ge(o_sq, 2 * b + t + 1)
                    if b == NB - 1:
                        mean_square_of(t, NB, NT + 2 * t + 1)
                    dve.tensor_tensor(o_tok[:, t, b * BLK:(b + 1) * BLK], bank[2 * (b % 2) + t][:, :],
                                      gain[:, b * BLK:(b + 1) * BLK], ALU.mult).then_inc(o_copied, 1)
                    if b == NB - 1:
                        if t == 1:
                            diagonal(0)
                        residual(t)
                if b < NB - 1:
                    rest_unit(dve, T_OUT + b, 6)
            diagonal(1)
            dve.sem_inc(up_free, START_FREE)
            dve.sem_inc(pr_done, 2)
            turn_lo(4, NB * NT, 0)
            turn_lo(0, NB * NT, 1)
            rest_unit(dve, T_OUT + NB - 1, 6)

            def finish(pp, h, p):
                dve.wait_ge(acth_done, pp + 1)
                dve.tensor_tensor(one(act_lo, pp - HALF * h), prod[p][:, :], one(act_hi, pp - HALF * h),
                                  ALU.subtract).then_inc(act_done, 1)

            def up(T0, j0, r, pp, h, first=False):
                p = (j0 // 2) % 2
                for i in range(2):
                    c = conv_o[p][i]
                    src = up_o[p][i]
                    both_halves(4 * h + 2 * p + i, src[:, :], up_lo, 2 * pp + i + 1, up_free)
                    rest_unit(dve, T0, j0 + i + 3, r)
                    dve.wait_ge(c_mid, 2 * pp + i + 1)
                    dve.scalar_tensor_tensor(c[:, 1:SEQ], src[:, 0:SEQ - 1], convw[:, bass.ds(pp, 1), i, 0], c[:, 1:SEQ],
                                             ALU.mult, ALU.add).then_inc(c_left, 1)
                    dve.wait_ge(c_left, 2 * pp + i + 1)
                    dve.scalar_tensor_tensor(c[:, 0:SEQ - 1], src[:, 1:SEQ], convw[:, bass.ds(pp, 1), i, 2], c[:, 0:SEQ - 1],
                                             ALU.mult, ALU.add).then_inc(c_done, 1)
                    if i == 0 and not first:
                        finish(pp - 1, h, 1 - p)
                dve.wait_ge(ge_done, pp + 1)
                dve.wait_ge(c_done, 2 * pp + 2)
                dve.tensor_tensor(prod[p][:, :], gelu_o[p][:, :], conv_o[p][1][:, :], ALU.mult).then_inc(pr_done, 1)

            def f_block(h, n, tiles=range(NT), blocks=range(2)):
                for t in tiles:
                    if (h, n) != (1, 1):
                        dve.wait_ge(w_used, RING * (T_FFN + h * HALF_TURNS + UP_TURNS + (n + 1) * DOWN_TURNS))
                    for c in blocks:
                        if (h, n) == (1, 1):
                            dve.wait_ge(f_ready, 2 * t + c + 1)
                        col = slice((2 * n + c) * BLK, (2 * n + c + 1) * BLK)
                        src = bank[down_bank(h, n) + 2 * t + c]
                        if h == 0:
                            dve.tensor_copy(f_tok[:, t, col], src[:, :]).then_inc(f_done, 1)
                        else:
                            dve.wait_ge(f_done, 4 * n + 2 * t + c + 1)
                            dve.tensor_tensor(f_tok[:, t, col], f_tok[:, t, col], src[:, :], ALU.add).then_inc(f_done, 1)

            for h in range(2):
                T0 = T_FFN + h * HALF_TURNS
                for q in range(2):
                    up(T0, 2 * q, 0, q + HALF * h, h, first=q == 0)
                with dve.Fori(1, UP_TURNS) as i:
                    for q in range(2):
                        up(T0, 2 * q, i, 2 * i + q + HALF * h, h)
                finish(HALF * (h + 1) - 1, h, 1)
                for n in range(2):
                    for j in range(DOWN_TURNS * RING):
                        rest_unit(dve, T0 + UP_TURNS + n * DOWN_TURNS, j + 3)
                        if j == 0 and n == 1:
                            f_block(h, 0)
                if h == 0:
                    f_block(h, 1)
            dve.wait_ge(last_gain_in, 16)
            for t in range(NT):
                for c in range(2):
                    f_block(1, 1, [t], [c])
                    col = slice((2 + c) * BLK, (3 + c) * BLK)
                    dve.wait_ge(f_sq, 4 + 2 * t + c + 1)
                    if c == 1:
                        mean_square_of(t, NB, 3 * NT + t + 1)
                    dve.tensor_tensor(f_tok[:, t, col], f_tok[:, t, col], gain[:, col], ALU.mult).then_inc(fg_dve, 1)
                dve.wait_ge(rstd_done, N_LAST[t] + 1)
                dve.wait_ge(fg_pool, 2 * t + 2)
                dve.wait_ge(fg_dve, 2 * t + 2)
                for b in range(NB):
                    col = slice(b * BLK, (b + 1) * BLK)
                    dve.scalar_tensor_tensor(f_tok[:, t, col], f_tok[:, t, col], rstd[:, t:t + 1], x_tok[:, t, col],
                                             ALU.mult, ALU.add).then_inc(y_done, 1)

        @block.tensor
        def _(pe):
            def passes(dst, a_hi, a_lo, b_hi, b_lo, first, last):
                pe.matmul(dst, a_hi, b_hi, start=first, stop=False)
                pe.matmul(dst, a_hi, b_lo, start=False, stop=False)
                return pe.matmul(dst, a_lo, b_hi, start=False, stop=last)

            def arrived(T0, j, r=0):
                pe.wait_ge(wl_ready, (T0 + r) * RING + j + 1)

            def product(T0, j, r, dst, rhs, ks=range(KD), turned=0, done=True):
                hi = w_hi[j % RING][:, :].rearrange("p (k m) -> p k m", m=P)
                lo = w_lo[j % RING][:, :].rearrange("p (k m) -> p k m", m=P)
                for k in ks:
                    i = k - ks[0]
                    if turned and k % 4 == 0:
                        pe.wait_ge(hl_done, turned + k // 4 + 1)
                    pe.matmul(dst[:, :].rearrange("p (a s) -> p a s", a=2), hi[:, k, :], rhs[:, :, i, :],
                              start=i == 0, stop=False)
                    last = pe.matmul(dst[:, 0:SEQ], lo[:, k, :], rhs[:, 0, i, :], start=False, stop=i == len(ks) - 1)
                if done:
                    last.then_inc(w_used, 1)

            def tokens(T0, banks, src_hi, src_lo, waits=None, ready=None, order=None):
                for t, c in order or [(t, c) for t in range(NT) for c in range(RING)]:
                    if t == 0:
                        arrived(T0, c)
                    if waits:
                        waits(t, c)
                    hi = w_hi[c][:, :].rearrange("p (k n) -> p k n", n=BLK)
                    lo = w_lo[c][:, :].rearrange("p (k n) -> p k n", n=BLK)
                    for kk in range(4):
                        k = 4 * c + kk
                        tt = slice(t * P, (t + 1) * P)
                        last = passes(banks[t][:, :], src_hi[:, k, tt], src_lo[:, k, tt], hi[:, kk, :], lo[:, kk, :],
                                      k == 0, k == KD - 1)
                    if t == NT - 1:
                        last.then_inc(w_used, 1)
                    elif ready is not None and c == RING - 1:
                        last.then_inc(ready, 1)

            def turn_block(src, first_bank, t, b, rhs):
                for k in range(4):
                    dst = bank[first_bank + b][:, k * P:(k + 1) * P]
                    part = src[:, t, (4 * b + k) * P:(4 * b + k + 1) * P]
                    if rhs is ident:
                        last = pe.transpose(dst, part, ident[:, :])
                    else:
                        last = pe.matmul(dst, part, rhs[:, :], start=True, stop=True)
                last.then_inc(tr_done, 1)

            def scores(h, p, guard=True):
                pe.wait_ge(rope_done, NKV + h + 1)
                if guard:
                    pe.wait_ge(sc_read, h)
                g = kv_of(h, p)
                for t in range(NT):
                    last = pe.matmul(bank[4][:, t * SEQ:(t + 1) * SEQ], qT[p][:, t * P:(t + 1) * P], g, start=True, stop=True)
                last.then_inc(sc_ready, 1)

            def kv_of(h, p):
                return kT[:, bass.ds(h // QPK, 1), :].rearrange("p g s -> p (g s)")

            def turn_probs(h, p):
                pe.wait_ge(p_ready, 2 * h + 2)
                pe.wait_ge(pt_free, h + 1)
                for t in range(NT):
                    for k in range(NT):
                        last = pe.transpose(bank[5][:, k * SEQ + t * P:k * SEQ + (t + 1) * P],
                                            prob[p][:, t, k * P:(k + 1) * P], ident[:, :])
                last.then_inc(pt_ready, 1)

            def values(h, g):
                pe.wait_ge(pt_free, h + 2)
                pe.wait_ge(bl_free, h + 1)
                for k in range(NT):
                    last = pe.matmul(bank[6][:, 0:SEQ], v_tok[:, k, g * P:(g + 1) * P], pT[:, k, :],
                                     start=k == 0, stop=k == NT - 1)
                last.then_inc(pv_ready, 1)

            def spatial(h, guard=True):
                if guard:
                    pe.wait_ge(vz_done, h)
                for c in range(NT):
                    last = pe.matmul(bank[7][:, c * P:(c + 1) * P], vg[:, c, h * P:(h + 1) * P], sgw[:, h, :],
                                     start=True, stop=True)
                last.then_inc(vz_ready, 1)

            def head(h, T0):
                p = h % 2
                r = h // 2
                arrived(T0, 2 * p, r)
                if h >= 2:
                    pe.wait_ge(qk_summed, NKV + h - 1)
                product(T0, 2 * p, r, bank[p], hT)
                if h >= 1:
                    scores(h - 1, 1 - p, guard=h >= 2)
                if h >= 2:
                    turn_probs(h - 2, p)
                arrived(T0, 2 * p + 1, r)
                if h >= 2:
                    pe.wait_ge(u_summed, h - 1)
                product(T0, 2 * p + 1, r, bank[2 + p], hT)
                if h == 0:
                    pe.wait_ge(vt_done, NT)
                    pe.wait_ge(qk_summed, NKV)
                    pe.wait_ge(vn_done, NT)
                    pe.wait_ge(sg_in, 16 * 6)
                spatial(h, guard=h >= 1)
                if h >= 2:
                    values(h - 2, (h - 2) // QPK)

            pe.wait_ge(gain_in, 16)
            pe.wait_ge(ones_set, 1)
            for b in range(NB):
                pe.matmul(bank[4 + b][:, :], ones_row[:, :], gain_row[:, b * BLK:(b + 1) * BLK],
                          start=True, stop=True).then_inc(gain_rows, 1)
            pe.wait_ge(misc_in, 16)
            for b in range(NB):
                pe.wait_ge(xn_done, b + 1)
                turn_block(xn, 0, 0, b, ident)

            def v_waits(t, c):
                if (t, c) == (1, 0):
                    for b in range(NB):
                        pe.wait_ge(xn_done, NB + b + 1)
                        turn_block(xn, 4, 1, b, ident)
                pe.wait_ge(hl_done, NB * t + c + 1)
                if (t, c) == (0, 2):
                    pe.wait_ge(pool_lo, 1)

            tokens(0, bank[0:2], hT_hi, hT_lo, waits=v_waits,
                   order=[(0, 0), (0, 1), (1, 0), (1, 1), (0, 2), (1, 2), (0, 3), (1, 3)])
            tokens(1, bank[2:4], hT_hi, hT_lo)
            for c in range(2):
                arrived(T_KV, c)
                hi = w_hi[c][:, :].rearrange("p (k n) -> p k n", n=SEQ)
                lo = w_lo[c][:, :].rearrange("p (k n) -> p k n", n=SEQ)
                for kk in range(8):
                    k = 8 * c + kk
                    for t in range(NT):
                        tt = slice(t * P, (t + 1) * P)
                        last = passes(bank[4 + t][:, 0:SEQ], hT_hi[:, k, tt], hT_lo[:, k, tt], hi[:, kk, :], lo[:, kk, :],
                                      k == 0, k == KD - 1)
                last.then_inc(w_used, 1)
            for g in range(NKV):
                arrived(T_KV, 2 + g)
                product(T_KV, 2 + g, 0, bank[6 + g], hT)
            pe.wait_ge(vg_done, 2 * NT)
            for h in range(NH):
                head(h, T_QU)

            def branches(T0, j, r, p, guard):
                arrived(T0, j, r)
                if guard is not None:
                    pe.wait_ge(ab_sum, guard)
                product(T0, j, r, bank[4 + 2 * p], aT, ks=range(0, 8), done=False)
                product(T0, j, r, bank[5 + 2 * p], bT, ks=range(8, 16))

            def pair(T0, j0, r, n, first=False):
                for g in range(4):
                    arrived(T0, j0 + g, r)
                    if not first:
                        pe.wait_ge(gate_sum, 2 * n + g - 3)
                    else:
                        if g == 0:
                            pe.wait_ge(qk_summed, NKV + NH)
                        if g == 2:
                            pe.wait_ge(u_summed, NG)
                    product(T0, j0 + g, r, bank[g], hT)
                    if first and g == 0:
                        scores(NH - 1, 1)
                        turn_probs(NH - 2, 0)
                    if first and g == 1:
                        values(NH - 2, 1)
                        turn_probs(NH - 1, 1)
                    if first and g == 2:
                        values(NH - 1, 1)
                if first:
                    pe.wait_ge(bl_free, NH + 1)
                    pe.wait_ge(al_done, 1)
                for p in range(2):
                    branches(T0, j0 + 4 + p, r, p, None if first else 2 * (n + p) - 2)

            pair(T_MG, 0, 0, 0, first=True)
            pair(T_MG, 6, 0, 2)
            with pe.Fori(1, KD // 4) as i:
                pair(T_MG, 0, 3 * i, 4 * i)
                pair(T_MG, 6, 3 * i, 4 * i + 2)

            for b in range(NB):
                def o_waits(t, c):
                    if b == 0 and t == 0:
                        if c == 0:
                            pe.wait_ge(gate_sum, 2 * KD)
                        pe.wait_ge(ml_done, 4 * c + 4)
                    if b >= 2 and c == 0:
                        pe.wait_ge(o_copied, 2 * (b - 2) + t + 1)
                tokens(T_OUT + b, bank[2 * (b % 2):2 * (b % 2) + 2], mT_hi, mT_lo, waits=o_waits, ready=o_ready,
                       order=[(t, c) for c in range(RING) for t in range(NT)] if b == 0 else None)
            for t in range(NT):
                pe.wait_ge(diag_done, t + 1)
                for b in range(NB):
                    if b < 2:
                        pe.wait_ge(xg_pool, 2 * t + b + 1)
                    else:
                        pe.wait_ge(xg_dve, 2 * t + b - 1)
                    turn_block(o_tok, 4 * (1 - t), t, b, diag[t])

            def down(T1, j, h, first_bank, tiles=range(NT), blocks=range(2)):
                slot = j % RING
                if 0 in tiles and 0 in blocks:
                    arrived(T1, j)
                    pe.wait_ge(act_done, HALF * h + 2 * j + 2)
                hi = w_hi[slot][:, :].rearrange("p (k c n) -> p k c n", k=2, c=2)
                lo = w_lo[slot][:, :].rearrange("p (k c n) -> p k c n", k=2, c=2)
                for kk in range(2):
                    k = 2 * j + kk
                    first, final = k == 0, k == HALF - 1
                    for t in tiles:
                        tt = slice(t * P, (t + 1) * P)
                        dst = [bank[first_bank + 2 * t + c][:, :] for c in range(2)]
                        for c in blocks:
                            pe.matmul(dst[c], act_hi[:, k, tt], hi[:, kk, c, :], start=first, stop=False)
                        for c in blocks:
                            pe.matmul(dst[c], act_hi[:, k, tt], lo[:, kk, c, :], start=False, stop=False)
                        for c in blocks:
                            last = pe.matmul(dst[c], act_lo[:, k, tt], hi[:, kk, c, :], start=False, stop=final)
                if len(tiles) == NT:
                    last.then_inc(w_used, counts_for(T1 + j // RING, slot))
                return last

            for h in range(2):
                T0 = T_FFN + h * HALF_TURNS
                if h == 1:
                    pe.wait_ge(f_done, 4)
                with pe.Fori(0, UP_TURNS) as i:
                    for j in range(RING):
                        arrived(T0, j, i)
                        pe.wait_ge(up_free, (i + UP_TURNS * h) * RING + j + 1)
                        product(T0, j, i, bank[4 * h + j], hT,
                                          turned=NB * (2 * NT - 1) if (h, j) == (0, 0) else 0)
                for n in range(2):
                    T1 = T0 + UP_TURNS + n * DOWN_TURNS
                    first_bank = down_bank(h, n)
                    if n == 0 and h == 1:
                        pe.wait_ge(f_done, 8)
                    if n == 1:
                        pe.wait_ge(up_free, START_FREE + 2 * HALF * (h + 1))
                    split = DOWN_UNITS - RING if (h, n) == (1, 1) else DOWN_UNITS
                    for j in range(split):
                        down(T1, j, h, first_bank)
                    if split < DOWN_UNITS:
                        for t, blocks in ((0, [0, 1]), (1, [0]), (1, [1])):
                            for j in range(split, DOWN_UNITS):
                                last = down(T1, j, h, first_bank, [t], blocks)
                            last.then_inc(f_ready, len(blocks))


def _constants():
    import numpy as np
    ident = np.eye(P, dtype=np.float32)
    q = np.arange(P)[:, None, None] + P * np.arange(NT)[None, :, None]
    k = np.arange(SEQ)[None, None, :]
    mask = np.where(np.abs(k - q) <= P, 0.0, MASK_VALUE).astype(np.float32)
    pos = np.arange(SEQ, dtype=np.float32)
    inv = np.float32(ROPE_THETA) ** (-np.arange(0, ROT, 2, dtype=np.float32) / np.float32(ROT))
    ang = (pos[None, :] * inv[:, None]).astype(np.float32)
    cos, sin = np.cos(ang).astype(np.float32), np.sin(ang).astype(np.float32)
    rope = np.stack([np.concatenate([cos, cos]), np.concatenate([-sin, sin])], axis=1)
    return ident, mask, np.ascontiguousarray(rope)


def _pack(w_in, w_a, w_b, w_out, w_up, w_down):
    import numpy as np
    units = []

    def rows(w, k0, nk, c0, nc_):
        return w[k0 * P:(k0 + nk) * P, c0:c0 + nc_].reshape(nk, P, nc_).transpose(1, 0, 2)

    def add(*parts):
        units.append(np.concatenate([p.reshape(P, -1) for p in parts], axis=1))

    u0, v0, q0 = 0, SGW, 2 * SGW
    k0 = q0 + NH * P
    vv0 = k0 + NKV * P
    g0 = vv0 + NKV * P
    for b in range(SGW // BLK):
        for c in range(4):
            add(rows(w_in, 4 * c, 4, v0 + b * BLK, BLK))
    for c in range(2):
        add(rows(w_in, 8 * c, 8, vv0, NKV * P))
    for g in range(NKV):
        add(rows(w_in, 0, KD, k0 + g * P, P))
    for h in range(NH):
        add(rows(w_in, 0, KD, q0 + h * P, P))
        add(rows(w_in, 0, KD, u0 + h * P, P))
    for n0 in range(0, KD, 2):
        for n in (n0, n0 + 1):
            add(rows(w_in, 0, KD, g0 + n * P, P))
            add(rows(w_in, 0, KD, g0 + D + n * P, P))
        for n in (n0, n0 + 1):
            add(rows(w_a, 0, 8, n * P, P), rows(w_b, 0, 8, n * P, P))
    for b in range(NB):
        for c in range(4):
            add(rows(w_out, 4 * c, 4, b * BLK, BLK))
    for h in range(2):
        for i in range(HALF * h, HALF * (h + 1)):
            add(rows(w_up, 0, KD, i * P, P))
            add(rows(w_up, 0, KD, DFF + i * P, P))
        for n in range(2):
            for j in range(DOWN_UNITS):
                add(rows(w_down, HALF * h + 2 * j, 2, n * 1024, 1024))
    return np.stack(units)


def kernel(x, norm_mix_pre, w_in, sg_ln_g, sg_ln_b, sg_w, sg_b, attn_sink, w_branch_a, w_branch_b, w_out,
           norm_mix_post, norm_ffn_pre, w_up, conv_w, conv_b, w_down, norm_ffn_post):
    import numpy as np
    import concourse.bacc as bacc
    from concourse.bass_utils import run_bass_kernel_spmd as run

    a = {k: np.asarray(v) for k, v in dict(
        x=x, npre=norm_mix_pre, w_in=w_in, lg=sg_ln_g, lb=sg_ln_b, sg_w=sg_w, sg_b=sg_b, sink=attn_sink,
        wa=w_branch_a, wb=w_branch_b, wo=w_out, npost=norm_mix_post, nfpre=norm_ffn_pre, w_up=w_up,
        cw=conv_w, cb=conv_b, wd=w_down, nfpost=norm_ffn_post).items()}
    ident, mask, rope = _constants()
    taps = np.concatenate([a["cw"][0], a["cb"]], axis=0)
    conv = taps.reshape(4, 2, KF, P).transpose(3, 2, 1, 0)
    arrays = {
        "x": a["x"].reshape(NT, P, D),
        "weights": _pack(a["w_in"][0], a["wa"][0], a["wb"][0], a["wo"][0], a["w_up"][0], a["wd"][0]),
        "gains": np.concatenate([a["npre"], a["npost"], a["nfpre"], a["nfpost"]], axis=0),
        "sg_gb": np.concatenate([a["lg"], a["lb"]], axis=0),
        "sg_wT": a["sg_w"][0].transpose(2, 0, 1),
        "sg_b": a["sg_b"].reshape(1, NG, P),
        "sink": a["sink"].reshape(1, NH),
        "conv": conv,
        "ident": ident, "mask": mask, "rope": rope,
    }
    arrays = {k: np.ascontiguousarray(v) for k, v in arrays.items()}
    nc = bacc.Bacc("TRN2", target_bir_lowering=False, num_devices=1, dynamic_dma_scratch_size=1024)
    args = [nc.dram_tensor(k, v.shape, mybir.dt.from_np(v.dtype), kind="ExternalInput").ap() for k, v in arrays.items()]
    out = nc.dram_tensor("out", (NT, P, D), mybir.dt.float32, kind="ExternalOutput").ap()
    build(nc, *args, out)
    r = run(nc, [arrays], core_ids=[0])
    return r.results[0]["out"].reshape(1, SEQ, D)
```
